# Optimizing a Trainium2 kernel written in Bass

```python
import math
import jax, jax.numpy as jnp
from jax import lax
import numpy as np

D_MODEL = 1024
BATCH = 1
SEQ = 2048
DEPTH = 1

N_META = 16
RWKV_HEADS = 16
RWKV_HEAD_DIM = 64
RWKV_WIDTH = RWKV_HEADS * RWKV_HEAD_DIM
LORA_W = 64
LORA_A = 64
SB_HEADS = 16
SB_HEAD_DIM = 64
SB_WIDTH = SB_HEADS * SB_HEAD_DIM
SB_BLOCK = 128
N_BRANCH = 2
RWKV_SHIFT_COLS = 3 * RWKV_WIDTH + LORA_W + LORA_A
IN_SIZES = (RWKV_SHIFT_COLS, RWKV_WIDTH, SB_WIDTH, SB_WIDTH, SB_WIDTH, SB_WIDTH, N_BRANCH * D_MODEL)
IN_COLS = RWKV_SHIFT_COLS + RWKV_WIDTH + 4 * SB_WIDTH + N_BRANCH * D_MODEL
RMS_EPS = 1e-6
GN_EPS = 64e-5
L2_EPS = 1e-12
DECAY_SCALE = 0.6065306597126334

kernel_name = "hybrid_rwkv7_stickbreaking_gated_layer"

def _split(t, sizes):
    outs = []
    start = 0
    for size in sizes:
        outs.append(t[..., start:start + size])
        start += size
    return outs

def _rms_norm(t, g):
    t32 = t.astype(jnp.float32)
    inv = lax.rsqrt(jnp.mean(t32 * t32, axis=-1, keepdims=True) + RMS_EPS)
    return (t32 * inv * g.astype(jnp.float32)).astype(t.dtype)

def _heads(t, n_heads):
    return t.reshape(t.shape[:-1] + (n_heads, t.shape[-1] // n_heads))

def _rwkv7_step(state, inputs):
    r, decay, kk, a, k, v = inputs
    sa = jnp.einsum("bhvk,bhk->bhv", state, kk)
    state = (state * decay[:, :, None, :]
             - sa[..., None] * (kk * a)[:, :, None, :]
             + v[..., None] * k[:, :, None, :])
    y = jnp.einsum("bhvk,bhk->bhv", state, r)
    return state, y

def _rwkv7_time_mix(u, mu, w0, w_up, a0, a_up, k_k, k_a, r_k, gn_g, gn_b):
    bsz, length, _ = u.shape
    f32 = jnp.float32
    u_prev = jnp.pad(u, ((0, 0), (1, 0), (0, 0)))[:, :-1]
    u = u + (u_prev - u) * mu
    r, k, v, w_lo, a_lo = _split(u, (RWKV_WIDTH, RWKV_WIDTH, RWKV_WIDTH, LORA_W, LORA_A))
    decay = jnp.exp(-DECAY_SCALE * jax.nn.sigmoid((w0 + jnp.tanh(w_lo) @ w_up).astype(f32)))
    a = jax.nn.sigmoid((a0 + a_lo @ a_up).astype(f32))
    k = k.astype(f32)
    kk = _heads(k * k_k, RWKV_HEADS)
    kk = kk * lax.rsqrt(jnp.sum(kk * kk, axis=-1, keepdims=True) + L2_EPS)
    k = _heads(k * (1.0 + (a - 1.0) * k_a), RWKV_HEADS)
    r = _heads(r.astype(f32), RWKV_HEADS)
    v = _heads(v.astype(f32), RWKV_HEADS)
    decay = _heads(decay, RWKV_HEADS)
    a = _heads(a, RWKV_HEADS)
    state0 = jnp.zeros((bsz, RWKV_HEADS, RWKV_HEAD_DIM, RWKV_HEAD_DIM), f32)
    xs = tuple(jnp.moveaxis(t, 1, 0) for t in (r, decay, kk, a, k, v))
    _, y = lax.scan(_rwkv7_step, state0, xs)
    y = jnp.moveaxis(y, 0, 1)
    mean = jnp.mean(y, axis=-1, keepdims=True)
    var = jnp.mean(jnp.square(y - mean), axis=-1, keepdims=True)
    y = ((y - mean) * lax.rsqrt(var + GN_EPS)).reshape(bsz, length, RWKV_WIDTH) * gn_g + gn_b
    bonus = jnp.sum(r * k * r_k, axis=-1, keepdims=True) * v
    return (y + bonus.reshape(bsz, length, RWKV_WIDTH)).astype(u.dtype)

def _stick_breaking_attention(q, k, v):
    length = q.shape[2]
    scale = SB_HEAD_DIM ** -0.5
    starts = [0] + list(range(N_META, length, SB_BLOCK))
    ends = starts[1:] + [length]
    outs = []
    for qs, qe in zip(starts, ends):
        logits = jnp.einsum("bhqd,bhkd->bhqk", q[:, :, qs:qe], k[:, :, :qe]).astype(jnp.float32) * scale
        visible = jnp.arange(qe)[None, :] < jnp.arange(qs, qe)[:, None]
        log_keep = jnp.where(visible, jax.nn.log_sigmoid(-logits), 0.0)
        log_between = lax.cumsum(log_keep, axis=3, reverse=True) - log_keep
        weights = jnp.where(visible, jnp.exp(jax.nn.log_sigmoid(logits) + log_between), 0.0)
        outs.append(jnp.einsum("bhqk,bhkd->bhqd", weights.astype(v.dtype), v[:, :, :qe]))
    return jnp.concatenate(outs, axis=2)

def setup_inputs(seed: int = 0) -> dict:
    key = jax.random.key(seed)
    ks = jax.random.split(key, 18)
    f32 = jnp.float32

    def nrm(k, shape, s):
        return jax.random.normal(k, shape, f32) * s

    return {
        "x": nrm(ks[0], (BATCH, SEQ, D_MODEL), 1.0),
        "meta_tokens": nrm(ks[1], (N_META, D_MODEL), 1.0),
        "pre_norm_g": 1.0 + nrm(ks[2], (DEPTH, D_MODEL), 0.05),
        "post_norm_g": 1.0 + nrm(ks[3], (DEPTH, D_MODEL), 0.05),
        "w_in": nrm(ks[4], (DEPTH, D_MODEL, IN_COLS), D_MODEL ** -0.5),
        "rwkv_mu": jax.random.uniform(ks[5], (DEPTH, RWKV_SHIFT_COLS), f32),
        "rwkv_w0": nrm(ks[6], (DEPTH, RWKV_WIDTH), 0.5),
        "rwkv_w_up": nrm(ks[7], (DEPTH, LORA_W, RWKV_WIDTH), 0.5 * LORA_W ** -0.5),
        "rwkv_a0": nrm(ks[8], (DEPTH, RWKV_WIDTH), 0.5),
        "rwkv_a_up": nrm(ks[9], (DEPTH, LORA_A, RWKV_WIDTH), 0.5 * LORA_A ** -0.5),
        "rwkv_k_k": 0.85 + nrm(ks[10], (DEPTH, RWKV_WIDTH), 0.05),
        "rwkv_k_a": 1.0 + nrm(ks[11], (DEPTH, RWKV_WIDTH), 0.05),
        "rwkv_r_k": nrm(ks[12], (DEPTH, RWKV_HEADS, RWKV_HEAD_DIM), 0.1),
        "rwkv_gn_g": 1.0 + nrm(ks[13], (DEPTH, RWKV_WIDTH), 0.05),
        "rwkv_gn_b": nrm(ks[14], (DEPTH, RWKV_WIDTH), 0.02),
        "w_proj_rwkv": nrm(ks[15], (DEPTH, RWKV_WIDTH, D_MODEL), RWKV_WIDTH ** -0.5),
        "w_proj_sb": nrm(ks[16], (DEPTH, SB_WIDTH, D_MODEL), SB_WIDTH ** -0.5),
        "w_out": nrm(ks[17], (DEPTH, D_MODEL, D_MODEL), D_MODEL ** -0.5),
    }

def reference(x, meta_tokens, pre_norm_g, post_norm_g, w_in, rwkv_mu, rwkv_w0, rwkv_w_up,
              rwkv_a0, rwkv_a_up, rwkv_k_k, rwkv_k_a, rwkv_r_k, rwkv_gn_g, rwkv_gn_b,
              w_proj_rwkv, w_proj_sb, w_out):
    bsz = x.shape[0]
    meta = jnp.broadcast_to(meta_tokens[None].astype(x.dtype), (bsz, N_META, D_MODEL))
    h = jnp.concatenate([meta, x], axis=1)
    length = h.shape[1]
    for l in range(DEPTH):
        hn = _rms_norm(h, pre_norm_g[l])
        proj = hn @ w_in[l]
        u_rwkv, g_rwkv, q_sb, k_sb, v_sb, g_sb, merge_logits = _split(proj, IN_SIZES)

        y_rwkv = _rwkv7_time_mix(u_rwkv, rwkv_mu[l], rwkv_w0[l], rwkv_w_up[l], rwkv_a0[l],
                                 rwkv_a_up[l], rwkv_k_k[l], rwkv_k_a[l], rwkv_r_k[l],
                                 rwkv_gn_g[l], rwkv_gn_b[l]) * jax.nn.silu(g_rwkv)

        to_bhld = lambda t: jnp.transpose(_heads(t, SB_HEADS), (0, 2, 1, 3))
        o_sb = _stick_breaking_attention(to_bhld(q_sb), to_bhld(k_sb), to_bhld(v_sb))
        y_sb = jnp.transpose(o_sb, (0, 2, 1, 3)).reshape(bsz, length, SB_WIDTH) * jax.nn.silu(g_sb)

        gate_rwkv, gate_sb = _split(jax.nn.sigmoid(merge_logits), (D_MODEL, D_MODEL))
        mixed = gate_rwkv * (y_rwkv @ w_proj_rwkv[l]) + gate_sb * (y_sb @ w_proj_sb[l])
        h = h + _rms_norm(mixed @ w_out[l], post_norm_g[l])
    return h[:, N_META:]


_drawn_inputs = setup_inputs


def setup_inputs(seed=0):
    import zlib

    import numpy as np

    out = dict(_drawn_inputs(seed))
    spreads = {}
    factors = {'rwkv_k_k': 7.411, 'rwkv_gn_b': 4.931}
    for name, (base, spread) in spreads.items():
        noise = np.random.default_rng([zlib.crc32(name.encode()), seed]).standard_normal(out[name].shape)
        drawn = base * np.exp(spread * noise) if base else spread * noise
        out[name] = __import__('jax').numpy.asarray(drawn.astype(out[name].dtype))
    for name, factor in factors.items():
        out[name] = (out[name] * factor).astype(out[name].dtype)
    return out
```

```python
from contextlib import ExitStack

import concourse.bass as bass
from concourse import mybir

ALU = mybir.AluOpType
ACT = mybir.ActivationFunctionType
F32 = mybir.dt.float32
F32R = mybir.dt.float32r

P = 128
D = 1024
SEQ = 2048
META = 16
HEADS = 16
DH = 64
PAIRS = HEADS // 2
KC = D // P
CHUNK = 64
PAD = CHUNK - META
TOK = PAD + META + SEQ
NCH = TOK // CHUNK
RMS_EPS = 1e-6
GN_EPS = 64e-5
L2_EPS = 1e-12
DECAY_SCALE = 0.6065306597126334

WB = 256
GS = [424, 424, 424, 424, 416]
GR = [512] * 4
STREAM, SILU, SIGMOID, TOKENS = range(4)
SEGMENTS = [
    (0, 12, STREAM, "u", 0),
    (16, 8, STREAM, "qk", 0),
    (12, 4, SILU, "gates", 0),
    (28, 4, SILU, "gates", D),
    (32, 8, SIGMOID, "merge", 0),
    (24, 4, TOKENS, "v_sb", 0),
]


def starts(sizes, at):
    out = []
    for s in sizes:
        out.append((at, s))
        at += s
    return out


def norm_phase(nc, sem, t, io):
    with ExitStack() as ctx:
        sb = lambda name, shape, dt=F32: ctx.enter_context(nc.sbuf_tensor(name, shape, dt))
        x = [sb(f"x{b}", [P, D]) for b in range(2)]
        hn = [sb(f"hn{b}", [P, D]) for b in range(2)]
        gained = [sb(f"gained{b}", [P, KC, P]) for b in range(2)]
        ssum = [sb(f"ssum{b}", [P, 1]) for b in range(2)]
        std = [sb(f"std{b}", [P, 1]) for b in range(2)]
        rinv = [sb(f"rinv{b}", [P, 1]) for b in range(2)]
        pt = [ctx.enter_context(nc.psum_tensor(f"pt{b}", [P, KC, P], F32)) for b in range(2)]
        const_in, zeroed = sem("n_const_in"), sem("n_zeroed")
        x_in = [sem(f"n_x_in{b}") for b in range(2)]
        summed, rooted, inverted, normed = sem("n_summed"), sem("n_rooted"), sem("n_inverted"), sem("n_normed")
        turned, gain_done, high_done, low_done = sem("n_turned"), sem("n_gain"), sem("n_high"), sem("n_low")
        block = ctx.enter_context(nc.Block())

        def tiles(eng, step):
            step(0, 1, CHUNK, 0)
            with eng.Fori(0, SEQ // P // 2) as i:
                for b in range(2):
                    step(1 + 2 * i + b, b, P, CHUNK + P * (2 * i + b))

        @block.sync
        def _(sp):
            sp.dma_start(t["identity"][:, :], io["identity"]).then_inc(const_in, 16)
            sp.dma_start(t["pre_g"][:, :], io["pre_norm_g"]).then_inc(const_in, 16)
            sp.wait_ge(zeroed, 1)
            sp.dma_start(x[1][PAD:CHUNK, :], io["meta_tokens"]).then_inc(x_in[1], 16)
            sp.dma_start(x[0][:, :], io["x"][0:P, :]).then_inc(x_in[0], 16)
            sp.wait_ge(normed, 1)
            sp.dma_start(x[1][:, :], io["x"][P:2 * P, :]).then_inc(x_in[1], 16)
            with sp.Fori(1, SEQ // P // 2) as i:
                for b in range(2):
                    sp.wait_ge(normed, 2 * i + b)
                    sp.dma_start(x[b][:, :], io["x"][bass.ds(P * (2 * i + b), P), :]).then_inc(x_in[b], 16)

        @block.scalar
        def _(act):
            def step(n, b, m, tok):
                act.wait_ge(x_in[b], 16 * (n // 2) + 16)
                act.activation(hn[b][0:m, :], x[b][0:m, :], ACT.Square, accum_out=ssum[b][0:m, :]).then_inc(summed, 1)
                act.wait_ge(summed, n + 1)
                act.activation(std[b][0:m, :], ssum[b][0:m, :], ACT.Sqrt, scale=1.0 / D,
                               bias=t["eps"][0:m, 0:1]).then_inc(rooted, 1)
                act.wait_ge(gain_done, n + 1)
                act.copy(t["hn_hi"][:, :, bass.ds(tok, m)], gained[b][:, :, 0:m]).then_inc(high_done, 1)

            act.wait_ge(zeroed, 3)
            tiles(act, step)

        @block.tensor
        def _(pe):
            def step(n, b, m, tok):
                pe.wait_ge(normed, n + 1)
                if not isinstance(n, int):
                    pe.wait_ge(gain_done, n)
                for k in range(KC):
                    mm = pe.transpose(pt[b][:, k, 0:m], hn[b][0:m, k * P:(k + 1) * P], t["identity"][0:m, 0:m])
                mm.then_inc(turned, 1)

            pe.wait_ge(const_in, 32)
            tiles(pe, step)

        @block.vector
        def _(dve):
            dve.memset(x[1][0:CHUNK, :], 0.0).then_inc(zeroed, 1)
            dve.memset(t["eps"][:, 0:1], RMS_EPS).then_inc(zeroed, 1)
            dve.memset(t["eps"][:, 1:2], GN_EPS).then_inc(zeroed, 1)
            dve.wait_ge(const_in, 32)

            def step(n, b, m, tok):
                dve.wait_ge(rooted, n + 1)
                dve.reciprocal(rinv[b][0:m, :], std[b][0:m, :]).then_inc(inverted, 1)
                dve.wait_ge(inverted, n + 1)
                dve.tensor_scalar(hn[b][0:m, :], x[b][0:m, :], rinv[b][0:m, 0:1], None, ALU.mult).then_inc(normed, 1)
                dve.wait_ge(turned, n + 1)
                for half in range(2):
                    ks = slice(4 * half, 4 * half + 4)
                    g = dve.tensor_tensor(gained[b][:, ks, 0:m], pt[b][:, ks, 0:m],
                                          t["pre_g"][:, ks].unsqueeze(2).broadcast_to([P, 4, m]), ALU.mult)
                g.then_inc(gain_done, 1)
                dve.wait_ge(high_done, n + 1)
                dve.tensor_tensor(t["hn_lo"][:, :, bass.ds(tok, m)], gained[b][:, :, 0:m],
                                  t["hn_hi"][:, :, bass.ds(tok, m)].bitcast(F32), ALU.subtract).then_inc(low_done, 1)

            tiles(dve, step)


def project_phase(nc, sem, t, io, scratch):
    with ExitStack() as ctx:
        sb = lambda name, shape, dt=F32: ctx.enter_context(nc.sbuf_tensor(name, shape, dt))
        raw = [sb(f"w_raw{b}", [P, KC, WB]) for b in range(2)]
        hi = [sb(f"w_hi{b}", [P, KC, WB], F32R) for b in range(2)]
        lo = [sb(f"w_lo{b}", [P, KC, WB], F32R) for b in range(2)]
        stage = [sb(f"stage{b}", [P, 512]) for b in range(2)]
        zero = sb("zero_col", [P, 3 * KC + 1])
        bank = [ctx.enter_context(nc.psum_tensor(f"pp{b}", [P, 512], F32)) for b in range(2)]
        w_in = [sem(f"p_w_in{b}") for b in range(2)]
        high, low = sem("p_high"), sem("p_low")
        product, staged = sem("p_product"), sem("p_staged")
        sent = [sem(f"p_sent{b}") for b in range(2)]
        zeroed, zeros_sent = sem("p_zeroed"), sem("p_zeros_sent")
        block = ctx.enter_context(nc.Block())

        def groups(kind):
            if kind == TOKENS:
                return [(None, 0, CHUNK)] + [(None, CHUNK + P * k, P) for k in range(SEQ // P)]
            sizes = starts(GS, 0) if kind == STREAM else starts(GR, CHUNK)
            return [(m, at, n) for m in range(WB // P) for at, n in sizes]

        def walk(eng, step):
            step(0, 0, 0, STREAM, None, None)
            n0, q0 = 1, len(GS)
            for seg in SEGMENTS:
                first, count, kind, _, _ = seg
                per = len(groups(kind))
                with eng.Fori(0, count // 2) as i:
                    for u in range(2):
                        step(n0 + u + 2 * i, (n0 + u) % 2, (q0 + u * per, i * 2 * per), kind, 2 * i + u, seg)
                n0 += count
                q0 += count * per

        def number(q, g):
            if isinstance(q, int):
                return q + g, (q + g) % 2, (q + g) // 2
            base, moving = q
            return base + g + moving, (base + g) % 2, (base + g) // 2 + moving // 2

        def of_block(kind, n):
            return groups(STREAM)[:len(GS)] if isinstance(n, int) else groups(kind)

        @block.sync
        def _(sp):
            def step(n, b, q, kind, blk, seg):
                src = io["w_lora"] if seg is None else io["w_main"][bass.ds(seg[0] + blk, 1)].rearrange(
                    "o p k -> (o p) k")
                if not isinstance(n, int):
                    sp.wait_ge(low, n)
                sp.dma_start(raw[b][:, :, :], src.rearrange("p (k c) -> p k c", k=KC)).then_inc(w_in[b], 16)

            walk(sp, step)

        @block.vector
        def _(dve):
            dve.memset(zero[:, :], 0.0).then_inc(zeroed, 1)
            dve.sem_inc(low, 1)

            def step(n, b, q, kind, blk, seg):
                uses = 1 if isinstance(n, int) else (n + 2 - b) // 2
                dve.wait_ge(w_in[b], 16 * uses)
                if not isinstance(n, int):
                    margin = min(len(GS), len(groups(kind))) - 1
                    dve.wait_ge(product, q[0] + q[1] - margin)
                dve.tensor_copy(hi[b][:, :, :], raw[b][:, :, :]).then_inc(high, 1)
                dve.wait_ge(high, n + 1)
                dve.tensor_tensor(lo[b][:, :, :], raw[b][:, :, :], hi[b][:, :, :].bitcast(F32),
                                  ALU.subtract).then_inc(low, 1)

            walk(dve, step)

        @block.tensor
        def _(pe):
            def step(n, b, q, kind, blk, seg):
                pe.wait_ge(low, n + 2)
                for g, (m, at, size) in enumerate(of_block(kind, n)):
                    num, slot, uses = number(q, g)
                    if not isinstance(num, int):
                        pe.wait_ge(staged, num - 1)
                    elif num >= 2:
                        pe.wait_ge(staged, num - 1)
                    passes = [(hi, "hn_hi"), (hi, "hn_lo"), (lo, "hn_hi")]
                    for k in range(KC):
                        for w, h in passes:
                            acts = t[h][:, k, at:at + size]
                            if m is None:
                                out, lhs, rhs = bank[slot][0:size, 0:WB], acts, w[b][:, k, :]
                            else:
                                out, lhs, rhs = bank[slot][:, 0:size], w[b][:, k, m * P:(m + 1) * P], acts
                            first = k == 0 and (w, h) == passes[0]
                            last = k == KC - 1 and (w, h) == passes[2]
                            mm = pe.matmul(out, lhs, rhs, start=first, stop=last)
                    mm.then_inc(product, 1)

            walk(pe, step)

        @block.scalar
        def _(act):
            act.wait_ge(zeroed, 1)
            act.dma_start(scratch["u"][:, 0:1].rearrange("(k p) c -> p k c", p=P), zero[:, :].unsqueeze(2),
                          allow_slow_non_contiguous=True).then_inc(zeros_sent, 16)

            def step(n, b, q, kind, blk, seg):
                for g, (m, at, size) in enumerate(of_block(kind, n)):
                    num, slot, uses = number(q, g)
                    act.wait_ge(product, num + 1)
                    if not isinstance(num, int) or num >= 2:
                        act.wait_ge(sent[slot], 16 * uses)
                    rows, cols = (size, WB) if m is None else (P, size)
                    func = {STREAM: ACT.Copy, TOKENS: ACT.Copy, SILU: ACT.Silu, SIGMOID: ACT.Sigmoid}[kind]
                    act.activation(stage[slot][0:rows, 0:cols], bank[slot][0:rows, 0:cols], func).then_inc(staged, 1)
                    act.wait_ge(staged, num + 1)
                    if seg is None:
                        dst = scratch["u"][3 * D:3 * D + P, 1 + at:1 + at + size]
                    elif m is None:
                        dst = scratch["v_sb"][at:at + size, bass.ds(blk * WB, WB)]
                    else:
                        off = {"u": 1 + at, "qk": at}.get(seg[3], at - CHUNK)
                        dst = scratch[seg[3]][bass.ds(blk * WB + seg[4] + m * P, P), off:off + size]
                    act.dma_start(dst, stage[slot][0:rows, 0:cols]).then_inc(sent[slot], 16)

            walk(act, step)
            total = len(GS) + sum(c * len(groups(k)) for _, c, k, _, _ in SEGMENTS)
            act.wait_ge(zeros_sent, 16)
            for slot in range(2):
                act.wait_ge(sent[slot], 16 * ((total + 1 - slot) // 2))


QT = SEQ // P
GROUP = 4
GROUPS = QT // GROUP
HIDDEN = -1e30


def keys_of(qt):
    return META + P * (qt + 1)


def pieces_of(qt):
    out, end = [], keys_of(qt)
    while end:
        size = min(512, end)
        out.append((end - size, size))
        end -= size
    return out


def merged(slow, fast):
    out, a, b = [], 0, 0
    while a < len(slow) or b < len(fast):
        if b >= len(fast) or (a < len(slow) and a * len(fast) <= b * len(slow)):
            out.append(slow[a])
            a += 1
        else:
            out.append(fast[b])
            b += 1
    return out


def attention_schedule():
    logits, values = [], []
    nl = nv = 0
    for g in range(2 * GROUPS):
        rows = []
        for qt in range(GROUP * (g % GROUPS), GROUP * (g % GROUPS + 1)):
            for k0, size in pieces_of(qt):
                rows.append(("logits", g, qt, k0, size, nl))
                nl += 1
        logits.append(rows)
        rows = []
        for kt in range(-1, GROUP * (g % GROUPS + 1)):
            rows.append(("values", g, kt, nv))
            nv += 1
        values.append(rows)
    order = list(logits[0])
    for g in range(2 * GROUPS):
        order += merged(values[g], logits[g + 1] if g + 1 < 2 * GROUPS else [])
    return order, nl, nv

def finishing(order, last_values, lag):
    out, steps, due = [], 0, []
    for e in order:
        out.append(e)
        if e[0] == "values":
            steps += 1
            while due and steps >= due[0][1]:
                out.append(("sum", due.pop(0)[0]))
            if e[3] == last_values[e[1]]:
                due.append((e[1], steps + lag + 1))
    return out + [("sum", g) for g, _ in due]



def attention_phase(nc, sem, t, io, scratch):
    order, n_logits, n_values = attention_schedule()
    LAG, ZB, TB, KB = 2, 2, 4, 4
    assert n_logits % ZB == n_logits % KB == n_values % TB == 0
    last_logits = {e[1]: e[5] for e in order if e[0] == "logits"}
    last_values = {e[1]: e[3] for e in order if e[0] == "values"}
    with ExitStack() as ctx:
        sb = lambda name, shape, dt=F32: ctx.enter_context(nc.sbuf_tensor(name, shape, dt))
        ps = lambda name, shape: ctx.enter_context(nc.psum_tensor(name, shape, F32))
        q_raw, k_raw = sb("q_raw", [P, SEQ]), sb("k_raw", [P, META + SEQ])
        v_now, v_before = sb("v_now", [P, 1 + QT, DH]), sb("v_before", [P, 1 + QT, DH])
        v_diff = sb("v_diff", [P, 1 + QT, DH])
        q_parts = [sb(f"q_parts{b}", [P, SEQ], F32R) for b in range(2)]
        k_high = [sb(f"k_high{b}", [P, META + SEQ], F32R) for b in range(2)]
        k_low = [sb(f"k_low{b}", [P, META + SEQ], F32R) for b in range(2)]
        dv = [sb(f"dv{b}", [P, 1 + QT, 2, DH], F32R) for b in range(2)]
        dv_diag = [sb(f"dv_diag{b}", [P, QT, 2, DH], F32R) for b in range(2)]
        longest = sum(keys_of(qt) for qt in range(QT - GROUP, QT))
        kept = [sb(f"kept{b}", [P, longest]) for b in range(2)]
        keep = [sb(f"keep{b}", [P, 512]) for b in range(KB)]
        w_high = [sb(f"w_high{b}", [P, 512], F32R) for b in range(TB)]
        w_low = [sb(f"w_low{b}", [P, 512], F32R) for b in range(TB)]
        low_half = sb("low_half", [DH, 512])
        total = sb("total", [DH, 512])
        gate = [sb(f"gate{b}", [DH, 512]) for b in range(2)]
        y = [sb(f"y_sb{b}", [DH, 512]) for b in range(2)]
        hidden, eye = sb("hidden", [P, P], F32R), sb("eye_r", [P, P], F32R)
        hidden_raw, last_row = sb("hidden_raw", [P, P]), sb("last_row", [P, 1])
        one = sb("one", [P, 1])
        z = [ps(f"z{b}", [P, 512]) for b in range(ZB)]
        turned = [ps(f"turned{b}", [P, 512]) for b in range(TB)]
        acc = [ps(f"acc{b}", [P, 512]) for b in range(2)]

        const_in, const_ready = sem("a_const_in"), sem("a_const_ready")
        raw_in, v_in = sem("a_raw_in"), sem("a_v_in")
        pool_step, head_ready = sem("a_pool_step"), sem("a_head_ready")
        logits_done, keep_done, scanned = sem("a_logits"), sem("a_keep"), sem("a_scanned")
        turn_done, high_done, low_done, value_done = sem("a_turned"), sem("a_high"), sem("a_low"), sem("a_values")
        half_done, total_done, y_done = sem("a_half"), sem("a_total"), sem("a_y")
        gate_in = [sem(f"a_gate_in{b}") for b in range(2)]
        y_sent = [sem(f"a_y_sent{b}") for b in range(2)]
        block = ctx.enter_context(nc.Block())
        GATES = 2 * GROUPS

        def done(per, i, k):
            return per * (i + 1) + k + 1

        def place(g, qt):
            return sum(keys_of(x) for x in range(GROUP * (g % GROUPS), qt))

        def key_tile(kt):
            return (0, META) if kt < 0 else (META + P * kt, P)

        def seen_by(g, kt):
            return max(0, kt - GROUP * (g % GROUPS))

        @block.sync
        def _(sp):
            sp.dma_start(hidden_raw[:, :], io["hidden"]).then_inc(const_in, 16)
            sp.dma_start(last_row[:, :], io["last_row"]).then_inc(const_in, 16)
            sp.wait_ge(const_ready, 2)
            with sp.Fori(0, HEADS) as head:
                sp.wait_ge(head_ready, head + 2)
                qrow, krow, cols = bass.ds(DH * head, DH), bass.ds(D + DH * head, DH), bass.ds(DH * head, DH)
                for half in range(2):
                    rows = slice(DH * half, DH * half + DH)
                    sp.dma_start(q_raw[rows, :], scratch["qk"][qrow, CHUNK:TOK]).then_inc(raw_in, 16)
                    sp.dma_start(k_raw[rows, :], scratch["qk"][krow, PAD:TOK]).then_inc(raw_in, 16)
                for shift, dst in ((0, v_now), (1, v_before)):
                    sp.dma_start(dst[0:META, 0, :], scratch["v_sb"][PAD - shift:CHUNK - shift, cols]).then_inc(v_in, 16)
                    sp.dma_start(dst[:, 1:, :], scratch["v_sb"][CHUNK - shift:TOK - shift, cols].rearrange(
                        "(k p) c -> p k c", p=P)).then_inc(v_in, 16)

        @block.gpsimd
        def _(pool):
            pool.sem_inc(head_ready, 2)
            pool.memset(v_now[:, 0, :], 0.0).then_inc(const_ready, 1)
            pool.memset(v_before[:, 0, :], 0.0).then_inc(const_ready, 1)
            pool.wait_ge(const_in, 32)
            pool.tensor_copy(hidden[:, :], hidden_raw[:, :]).then_inc(const_ready, 1)
            pool.memset(one[:, :], 1.0).then_inc(const_ready, 1)
            pool.wait_ge(const_ready, 4)
            pool.tensor_copy(eye[:, :], t["identity"][:, :]).then_inc(const_ready, 1)

            def rounded(out, x):
                ones = one[:, 0:1]
                for size in x.shape[1:-1]:
                    ones = ones.unsqueeze(1)
                return pool.tensor_tensor(out, x, ones.broadcast_to(x.shape), ALU.mult)

            with pool.Fori(0, PAIRS) as i:
                for u in range(2):
                    head = 2 * i + u
                    step = 10 * head
                    low = slice(DH, P)
                    pool.wait_ge(raw_in, 64 * head + 64)
                    pool.wait_ge(v_in, 64 * head + 64)
                    pool.wait_ge(value_done, done(n_values, i, last_values[GROUPS * (u + 1) - 1] - n_values))
                    pool.tensor_tensor(v_diff[:, :, :], v_before[:, :, :], v_now[:, :, :], ALU.subtract).then_inc(pool_step, 1)
                    pool.wait_ge(pool_step, step + 1)
                    rounded(dv[u][:, :, 0, :], v_diff[:, :, :]).then_inc(pool_step, 1)
                    pool.wait_ge(pool_step, step + 2)
                    pool.tensor_tensor(dv[u][:, :, 1, :], v_diff[:, :, :], dv[u][:, :, 0, :].bitcast(F32),
                                       ALU.subtract).then_inc(pool_step, 1)
                    pool.wait_ge(pool_step, step + 3)
                    pool.tensor_tensor(v_now[:, 1:, :], v_now[:, 1:, :],
                                       last_row[:, :].unsqueeze(1).broadcast_to([P, QT, DH]), ALU.mult).then_inc(pool_step, 1)
                    pool.wait_ge(pool_step, step + 4)
                    pool.tensor_tensor(v_diff[:, 1:, :], v_before[:, 1:, :], v_now[:, 1:, :], ALU.subtract).then_inc(pool_step, 1)
                    pool.wait_ge(pool_step, step + 5)
                    rounded(dv_diag[u][:, :, 0, :], v_diff[:, 1:, :]).then_inc(pool_step, 1)
                    pool.wait_ge(pool_step, step + 6)
                    pool.tensor_tensor(dv_diag[u][:, :, 1, :], v_diff[:, 1:, :], dv_diag[u][:, :, 0, :].bitcast(F32),
                                       ALU.subtract).then_inc(pool_step, 1)
                    pool.wait_ge(pool_step, step + 7)
                    rounded(q_parts[u][:, :], q_raw[:, :]).then_inc(pool_step, 1)
                    pool.wait_ge(pool_step, step + 8)
                    pool.tensor_tensor(q_parts[u][low, :], q_raw[low, :], q_parts[u][low, :].bitcast(F32),
                                       ALU.subtract).then_inc(pool_step, 1)
                    pool.wait_ge(pool_step, step + 9)
                    rounded(k_high[u][:, :], k_raw[:, :]).then_inc(pool_step, 1)
                    pool.wait_ge(pool_step, step + 10)
                    pool.tensor_tensor(k_low[u][:, :], k_raw[:, :], k_high[u][:, :].bitcast(F32),
                                       ALU.subtract).then_inc(head_ready, 1)

        @block.tensor
        def _(pe):
            pe.sem_inc(value_done, n_values)
            pe.sem_inc(turn_done, n_values)
            pe.wait_ge(const_ready, 5)
            with pe.Fori(0, PAIRS) as i:
                def logits(g, qt, k0, size, num):
                    u = g // GROUPS
                    pe.wait_ge(head_ready, done(2, i, u))
                    pe.wait_ge(keep_done, done(n_logits, i, num - ZB))
                    diagonal = k0 + size == keys_of(qt)
                    out = z[num % ZB][:, 0:size]
                    queries = q_parts[u][:, P * qt:P * qt + P]
                    pe.matmul(out, queries, k_high[u][:, k0:k0 + size], start=True, stop=False)
                    mm = pe.matmul(out, queries, k_low[u][:, k0:k0 + size], start=False, stop=not diagonal)
                    if diagonal:
                        mm = pe.matmul(z[num % ZB][:, size - P:size], eye[:, :], hidden[:, :], start=False, stop=True)
                    mm.then_inc(logits_done, 1)

                def turn(g, kt, num):
                    if kt < 0:
                        pe.wait_ge(scanned, done(n_logits, i, last_logits[g]))
                    pe.wait_ge(low_done, done(n_values, i, num - TB))
                    at, size = key_tile(kt)
                    for r in range(seen_by(g, kt), GROUP):
                        qt = GROUP * (g % GROUPS) + r
                        src = place(g, qt) + at
                        mm = pe.transpose(turned[num % TB][0:size, P * r:P * r + P], kept[g % 2][:, src:src + size],
                                          t["identity"][:, :])
                    mm.then_inc(turn_done, 1)

                def values(g, kt, num):
                    u, b = g // GROUPS, num % TB
                    pe.wait_ge(low_done, done(n_values, i, num))
                    if kt < 0:
                        pe.wait_ge(total_done, done(GATES, i, g - 2))
                    _, size = key_tile(kt)
                    r = seen_by(g, kt)
                    out = acc[g % 2]
                    own = kt - GROUP * (g % GROUPS) >= 0
                    last = kt == GROUP * (g % GROUPS + 1) - 1
                    c0 = P * r
                    for part in (w_high, w_low):
                        if own:
                            mm = pe.matmul(out[:, c0:c0 + P], dv_diag[u][:, kt, :, :], part[b][:, c0:c0 + P],
                                           start=False, stop=last and part is w_low)
                        c1 = c0 + P if own else c0
                        if c1 < 512:
                            mm = pe.matmul(out[:, c1:512], dv[u][0:size, kt + 1, :, :], part[b][0:size, c1:512],
                                           start=kt < 0 and part is w_high, stop=False)
                    mm.then_inc(value_done, 1)

                late = []
                for e in order:
                    if e[0] == "logits":
                        logits(*e[1:])
                    else:
                        turn(*e[1:])
                        late.append(e[1:])
                        if len(late) > LAG:
                            values(*late.pop(0))
                for e in late:
                    values(*e)

        @block.scalar
        def _(act):
            act.sem_inc(keep_done, n_logits)
            act.sem_inc(half_done, GATES)
            for b in range(2):
                act.sem_inc(y_sent[b], 16 * GROUPS)
            with act.Fori(0, PAIRS) as i:
                def load_gate(g):
                    rows = bass.ds(D + DH * (2 * i + g // GROUPS), DH)
                    at = 512 * (g % GROUPS)
                    act.wait_ge(y_done, done(GATES, i, g - 2))
                    act.dma_start(gate[g % 2][:, :], scratch["gates"][rows, at:at + 512]).then_inc(gate_in[g % 2], 16)

                def store_y(g):
                    rows = bass.ds(D + DH * (2 * i + g // GROUPS), DH)
                    at = 512 * (g % GROUPS)
                    act.wait_ge(y_done, done(GATES, i, g))
                    act.dma_start(scratch["y"][rows, at:at + 512], y[g % 2][:, :]).then_inc(y_sent[g % 2], 16)

                load_gate(0)
                load_gate(1)
                for e in finishing(order, last_values, LAG):
                    if e[0] == "logits":
                        _, g, qt, k0, size, num = e
                        act.wait_ge(logits_done, n_logits * i + num + 1)
                        act.wait_ge(scanned, done(n_logits, i, num - KB))
                        act.activation(keep[num % KB][:, 0:size], z[num % ZB][:, 0:size], ACT.Sigmoid,
                                       scale=-DH ** -0.5).then_inc(keep_done, 1)
                    elif e[0] == "values":
                        _, g, kt, num = e
                        _, size = key_tile(kt)
                        c0 = P * seen_by(g, kt)
                        act.wait_ge(turn_done, done(n_values, i, num))
                        act.wait_ge(value_done, done(n_values, i, num - TB))
                        act.copy(w_high[num % TB][0:size, c0:512], turned[num % TB][0:size, c0:512]).then_inc(high_done, 1)
                    else:
                        g = e[1]
                        act.wait_ge(value_done, done(n_values, i, last_values[g]))
                        act.wait_ge(total_done, done(GATES, i, g - 1))
                        act.copy(low_half[:, :], acc[g % 2][DH:P, :]).then_inc(half_done, 1)
                        if g >= 1:
                            store_y(g - 1)
                            if g + 1 < GATES:
                                load_gate(g + 1)
                store_y(GATES - 1)
            for b in range(2):
                act.wait_ge(y_sent[b], 16 * GROUPS * (PAIRS + 1))

        @block.vector
        def _(dve):
            dve.sem_inc(scanned, n_logits)
            dve.sem_inc(low_done, n_values)
            dve.sem_inc(total_done, GATES)
            dve.sem_inc(y_done, GATES)
            with dve.Fori(0, PAIRS) as i:
                for e in finishing(order, last_values, LAG):
                    if e[0] == "logits":
                        _, g, qt, k0, size, num = e
                        at = place(g, qt)
                        end = at + k0 + size
                        first = k0 + size == keys_of(qt)
                        dve.wait_ge(keep_done, done(n_logits, i, num))
                        if first and qt % GROUP == 0:
                            dve.wait_ge(turn_done, done(n_values, i, last_values[g - 2] if g >= 2 else
                                                        last_values[GATES + g - 2] - n_values))
                        if not first:
                            dve.wait_ge(scanned, done(n_logits, i, num - 1))
                        data = keep[num % KB][:, 0:size][:, ::-1]
                        dve.tensor_tensor_scan(kept[g % 2][:, end - size:end][:, ::-1], data, data,
                                               1.0 if first else kept[g % 2][:, end:end + 1],
                                               ALU.mult, ALU.bypass).then_inc(scanned, 1)
                    elif e[0] == "values":
                        _, g, kt, num = e
                        _, size = key_tile(kt)
                        c0 = P * seen_by(g, kt)
                        dve.wait_ge(high_done, n_values * i + num + 1)
                        dve.tensor_tensor(w_low[num % TB][0:size, c0:512], turned[num % TB][0:size, c0:512],
                                          w_high[num % TB][0:size, c0:512].bitcast(F32), ALU.subtract).then_inc(low_done, 1)
                    else:
                        g = e[1]
                        dve.wait_ge(half_done, done(GATES, i, g))
                        dve.tensor_tensor(total[:, :], acc[g % 2][0:DH, :], low_half[:, :], ALU.add).then_inc(total_done, 1)
                        dve.wait_ge(total_done, done(GATES, i, g))
                        dve.wait_ge(gate_in[g % 2], 16 * (GROUPS * i + g // 2 + 1))
                        dve.wait_ge(y_sent[g % 2], 16 * (GROUPS * (i + 1) + g // 2))
                        dve.tensor_tensor(y[g % 2][:, :], total[:, :], gate[g % 2][:, :], ALU.mult).then_inc(y_done, 1)


LEVELS = [2, 4, 8, 16, 32]
HALVES = 2
HP = PAIRS // HALVES
MU, MU_LORA, W0, A0, K_K, K_A, R_K, GN_G, GN_B = 0, 24, 25, 33, 41, 49, 57, 65, 73
N_PARAMS = 81


def rwkv_phase(nc, sem, t, io, scratch):
    with ExitStack() as ctx:
        sb = lambda name, shape, dt=F32: ctx.enter_context(nc.sbuf_tensor(name, shape, dt))
        C = CHUNK
        grid = [P, PAIRS, C]
        par, up = sb("par", [P, N_PARAMS]), sb("up", [P, D])
        omka_eps, eyes = sb("omka_eps", [P, 1]), sb("eyes", [P, HP * C])
        omka = sb("omka", [P, PAIRS])
        tri, full = sb("tri", [P, 8, C]), sb("full", [P, P])
        ones_sum, ones_mean, restart = sb("ones_sum", [P, P]), sb("ones_mean", [P, P]), sb("restart", [P, PAIRS * C])
        u_in, lora_in = sb("u_in", [P, 3 * PAIRS, C + 1]), sb("lora_in", [P, C + 1])
        gate, y_out = sb("gate", grid), sb("y_out", grid)
        rk_dif, rk = sb("rk_dif", [P, 2 * PAIRS, C]), sb("rk", [P, 2 * PAIRS, C])
        v_dif, v_mix = sb("v_dif", grid), sb("v_mix", grid)
        lora_dif, lora, lora_tanh = sb("lora_dif", [P, C]), sb("lora", [P, C]), sb("lora_tanh", [DH, C])
        logits, sig = sb("logits", [P, 2, PAIRS * C]), sb("sig", [P, 2, PAIRS, C])
        run, run_before = sb("run", [P, PAIRS * C]), sb("run_before", [P, PAIRS * C])
        w_now, w_inv, w_before = sb("w_now", grid), sb("w_inv", grid), sb("w_before", grid)
        w_end = sb("w_end", [P, PAIRS])
        kq, kq_sq, k_norm, k_rnorm, kk = sb("kq", grid), sb("kq_sq", grid), sb("k_norm", grid), sb("k_rnorm", grid), sb("kk", grid)
        k_gain, k_fin, r_bonus, kka = sb("k_gain", grid), sb("k_fin", grid), sb("r_bonus", grid), sb("kka", grid)
        bonus, bonus_v = sb("bonus", grid), sb("bonus_v", grid)
        AR, KB = sb("AR", [P, PAIRS, 2, C]), sb("KB", [P, PAIRS, 2, C])
        KBt = sb("KBt", [P, PAIRS, 2, DH])
        VU = sb("VU", [P, PAIRS, 2, DH])
        scores = sb("scores", [P, PAIRS, 2, 2, C])
        NT = sb("NT", grid)
        off = sb("off", [P, len(LEVELS), PAIRS, C])
        T2 = sb("T2", [P, HALVES, 2, HP, C])
        X = sb("X", grid)
        LV, R, S, S_sum = sb("LV", grid), sb("R", grid), sb("S", grid), sb("S_sum", grid)
        ysb, yc, yc_sq, y_std, y_rstd = sb("ysb", grid), sb("yc", grid), sb("yc_sq", grid), sb("y_std", grid), sb("y_rstd", grid)
        bank = [ctx.enter_context(nc.psum_tensor(f"rb{b}", [P, 512], F32)) for b in range(8)]

        def row(at, n=PAIRS, width=C):
            return par[:, at:at + n].unsqueeze(2).broadcast_to([P, n, width])

        def as_grid(b, n=PAIRS):
            return bank[b][:, 0:n * C].rearrange("p (k c) -> p k c", k=n)

        names = """pe_go const_in const_ready u_in_ready v_in_ready lora_in_ready gate_in y_sent
            rk_dif rk_scaled rk_mixed lora_dif lora_mixed tanh_done dve_logits logits_pe sig_done run_done run_before_done
            exp_done kq_done kq_sq_done norm_pe norm_done rnorm_done kk_done
            gain gain2 k_fin_done r_bonus1 r_bonus_done kka_done bonus_pe bonus_out bonus_v_done
            v_dif v_scaled v_mixed a_done r_done k_done b_done w_end_done
            kbt_pe kbt_out vt_pe vt_out nt_pe nt_out n_pe t_first t_init tt_first tt_init off_done
            st_pe st_out x_pe x_out t_pe t_out lv_pe lv_out r_pe r_out u_pe u_out0 u_out1 s_pe s_sum s_done
            y_pe ysb_out mean_pe yc_done yc_sq_done var_pe std_done rstd_done y_n1 y_n2 y_n3 y_n4 y_done"""
        s = {name: sem("r_" + name) for name in names.split()}
        block = ctx.enter_context(nc.Block())

        def ready(eng, name, n, k=0, per=1):
            eng.wait_ge(s[name], per * n + k + 1)

        def walk(eng, body, head=None, tail=None):
            if head:
                head()
            body(0, False, True)
            body(1, False, True)
            with eng.Fori(2, NCH - 1) as n:
                body(n, True, True)
            body(NCH - 1, True, False)
            if tail:
                tail()

        def out_of(n):
            return not (isinstance(n, int) and n == 0)

        def again(n):
            return not (isinstance(n, int) and n == 0)

        @block.sync
        def _(sp):
            sp.dma_start(par[:, :], io["params"]).then_inc(s["const_in"], 16)
            sp.dma_start(up[:, :], io["up"]).then_inc(s["const_in"], 16)
            sp.dma_start(tri[:, :, :], io["tri"].rearrange("p (k c) -> p k c", c=C)).then_inc(s["const_in"], 16)
            sp.dma_start(full[:, :], io["full"]).then_inc(s["const_in"], 16)
            sp.dma_start(ones_sum[:, :], io["ones_sum"]).then_inc(s["const_in"], 16)
            sp.dma_start(restart[:, :], io["restart"]).then_inc(s["const_in"], 16)

            def load(n):
                if again(n):
                    ready(sp, "rk_mixed", n - 1)
                src = scratch["u"][0:3 * D, bass.ds(C * n, C + 1)].rearrange("(k p) c -> p k c", p=P)
                sp.dma_start(u_in[:, 0:2 * PAIRS, :], src[:, 0:2 * PAIRS, :]).then_inc(s["u_in_ready"], 16)
                if again(n):
                    ready(sp, "v_mixed", n - 1)
                    ready(sp, "lora_mixed", n - 1)
                sp.dma_start(lora_in[:, :], scratch["u"][3 * D:3 * D + P, bass.ds(C * n, C + 1)]).then_inc(s["lora_in_ready"], 16)
                sp.dma_start(u_in[:, 2 * PAIRS:, :], src[:, 2 * PAIRS:, :]).then_inc(s["v_in_ready"], 16)

            def store(n):
                ready(sp, "y_done", n - 1)
                sp.dma_start(scratch["y"][0:D, bass.ds(C * n - C, C)].rearrange("(k p) c -> p k c", p=P),
                             y_out[:, :, :]).then_inc(s["y_sent"], 16)

            def load_gate(n):
                sp.dma_start(gate[:, :, :], scratch["gates"][0:D, bass.ds(C * n - C, C)].rearrange(
                    "(k p) c -> p k c", p=P)).then_inc(s["gate_in"], 16)

            def body(n, prev_out, prep):
                if prep:
                    load(n + 1)
                if prev_out:
                    store(n - 1)
                if out_of(n):
                    load_gate(n)

            def tail():
                store(NCH - 1)
                sp.wait_ge(s["y_sent"], 16 * (NCH - 1))

            walk(sp, body, lambda: load(0), tail)

        @block.tensor
        def _(pe):
            def low_rank(n):
                ready(pe, "tanh_done", n)
                ready(pe, "lora_mixed", n)
                if again(n):
                    ready(pe, "norm_done", n - 1)
                    if out_of(n - 1):
                        ready(pe, "bonus_out", n - 2)
                for k in range(PAIRS):
                    pe.matmul(bank[0][:, C * k:C * k + C], up[0:DH, P * k:P * k + P], lora_tanh[:, :],
                              start=True, stop=True)
                for k in range(PAIRS):
                    mm = pe.matmul(bank[1][:, C * k:C * k + C], up[DH:P, P * k:P * k + P], lora[DH:P, :],
                                   start=True, stop=True)
                mm.then_inc(s["logits_pe"], 1)

            def key_norm(n):
                ready(pe, "kq_sq_done", n)
                ready(pe, "dve_logits", n)
                pe.matmul(bank[0][:, :], ones_sum[:, :], kq_sq[:, :, :], start=True, stop=True).then_inc(s["norm_pe"], 1)

            def bonus_sum(n):
                ready(pe, "r_bonus_done", n)
                pe.matmul(bank[1][:, :], ones_sum[:, :], r_bonus[:, :, :], start=True, stop=True).then_inc(s["bonus_pe"], 1)

            def both(f):
                for k in range(PAIRS):
                    for h in range(2):
                        f(k, h, slice(DH * h, DH * h + DH))

            def go():
                pe.sem_inc(s["pe_go"], 1)

            def body(n, prev_out, prep):
                if again(n):
                    ready(pe, "s_done", n - 1)
                    if out_of(n - 1):
                        ready(pe, "ysb_out", n - 2, 1, 2)
                for name in ("v_mixed", "a_done", "r_done", "k_done", "b_done"):
                    ready(pe, name, n)
                for k in range(PAIRS):
                    mm = pe.transpose(bank[2 + k // HP][:, P * (k % HP):P * (k % HP) + P],
                                      KB[:, k, :, :].rearrange("p a c -> p (a c)"), t["identity"][:, :])
                mm.then_inc(s["kbt_pe"], 1)
                for k in range(PAIRS):
                    mm = pe.transpose(bank[4 + k // HP][0:C, P * (k % HP):P * (k % HP) + P], v_mix[:, k, :],
                                      t["identity"][:, :])
                mm.then_inc(s["vt_pe"], 1)
                if again(n):
                    ready(pe, "u_out0", n - 1, 1, 2)
                    ready(pe, "u_out1", n - 1, 1, 2)
                    go()
                for k in range(PAIRS):
                    for h in range(2):
                        hs = slice(DH * h, DH * h + DH)
                        mm = pe.matmul(bank[6][hs, C * k:C * k + C], KB[hs, k, 1, :], AR[hs, k, 0, :], start=True, stop=True)
                mm.then_inc(s["nt_pe"], 1)
                for k in range(PAIRS):
                    for h in range(2):
                        hs = slice(DH * h, DH * h + DH)
                        mm = pe.matmul(bank[7][hs, C * k:C * k + C], AR[hs, k, 0, :], KB[hs, k, 1, :], start=True, stop=True)
                mm.then_inc(s["n_pe"], 1)
                ready(pe, "kbt_out", n, 1, 2)
                for half in range(HALVES):
                    if half:
                        ready(pe, "vt_out", n, 1, 2)
                    for h in range(2):
                        hs = slice(DH * h, DH * h + DH)
                        for k in range(HP):
                            kk_ = HP * half + k
                            mm = pe.matmul(bank[2 + 2 * half + h][:, P * k:P * k + P],
                                           KB[hs, kk_, :, :].rearrange("p a c -> p (a c)"),
                                           AR[hs, kk_, :, :].rearrange("p a c -> p (a c)"), start=True, stop=True)
                        mm.then_inc(s["st_pe"], 1)
                if out_of(n):
                    bonus_sum(n)

                ready(pe, "t_init", n)
                ready(pe, "tt_init", n)
                ready(pe, "st_out", n, 3, 4)
                for lv in range(len(LEVELS)):
                    last = lv == len(LEVELS) - 1
                    ready(pe, "off_done", n, lv, len(LEVELS))
                    for half in range(HALVES):
                        if lv:
                            ready(pe, "t_out", n, 2 * (lv - 1) + half, 10)
                        go()
                        for k in range(HP):
                            for h in range(2):
                                hs = slice(DH * h, DH * h + DH)
                                mm = pe.matmul(bank[2 + half][hs, C * k:C * k + C], off[hs, lv, HP * half + k, :],
                                               T2[hs, half, 0, k, :], start=True, stop=True)
                        mm.then_inc(s["x_pe"], 1)
                    for half in range(HALVES):
                        ready(pe, "x_out", n, 2 * lv + half, 10)
                        go()
                        for k in range(HP):
                            for h in range(2):
                                hs = slice(DH * h, DH * h + DH)
                                x = X[hs, HP * half + k, :]
                                if not last:
                                    pe.matmul(bank[4 + half][hs, C * k:C * k + C], T2[hs, half, 1, k, :], x,
                                              start=True, stop=True)
                                mm = pe.matmul(bank[4 + half][hs, C * (HP + k):C * (HP + k) + C], x,
                                               T2[hs, half, 1, k, :], start=True, stop=True)
                        mm.then_inc(s["t_pe"], 1)
                    if lv == 0 and prev_out:
                        ready(pe, "ysb_out", n - 2, 1, 2)
                        ready(pe, "nt_out", n)
                        pe.matmul(bank[6][:, :], ones_mean[:, :], ysb[:, :, :], start=True, stop=True).then_inc(s["mean_pe"], 1)
                    if lv == 1 and prep:
                        low_rank(n + 1)
                    if lv == 2:
                        if prev_out:
                            ready(pe, "yc_sq_done", n - 2)
                            pe.matmul(bank[7][:, :], ones_mean[:, :], yc_sq[:, :, :], start=True, stop=True).then_inc(s["var_pe"], 1)
                        if prep:
                            key_norm(n + 1)

                if prev_out:
                    ready(pe, "yc_done", n - 2)
                ready(pe, "vt_out", n, 1, 2)
                go()
                for k in range(PAIRS):
                    for h in range(2):
                        mm = pe.matmul(bank[6][DH * h:DH * h + DH, C * k:C * k + C], scores[0:DH, k, h, 0, :],
                                       VU[0:DH, k, h, :], start=True, stop=True)
                mm.then_inc(s["lv_pe"], 1)
                for half in range(HALVES):
                    for k in range(HP):
                        for h in range(2):
                            hs = slice(DH * h, DH * h + DH)
                            mm = pe.matmul(bank[2 + half][hs, C * k:C * k + C], AR[hs, HP * half + k, 0, :],
                                           S[hs, HP * half + k, :], start=True, stop=True)
                    mm.then_inc(s["r_pe"], 1)
                ready(pe, "lv_out", n)
                if prev_out:
                    ready(pe, "std_done", n - 2)
                for half in range(HALVES):
                    ready(pe, "r_out", n, half, 2)
                    ready(pe, "t_out", n, 9, 10)
                    go()
                    for h in range(2):
                        hs = slice(DH * h, DH * h + DH)
                        for k in range(HP):
                            mm = pe.matmul(bank[4 + 2 * half + h][DH:P, C * k:C * k + C], T2[hs, half, 1, k, :],
                                           R[hs, HP * half + k, :], start=True, stop=True)
                    mm.then_inc(s["u_pe"], 1)
                for half in range(HALVES):
                    ready(pe, "u_out0", n, half, 2)
                    ready(pe, "u_out1", n, half, 2)
                    for k in range(HP):
                        for h in range(2):
                            mm = pe.matmul(bank[2 + half][DH * h:DH * h + DH, C * k:C * k + C], KBt[:, HP * half + k, h, :],
                                           VU[:, HP * half + k, h, :], start=True, stop=True)
                    mm.then_inc(s["s_pe"], 1)
                if out_of(n):
                    for half in range(HALVES):
                        for k in range(HP):
                            for h in range(2):
                                hs = slice(DH * h, DH * h + DH)
                                kk_ = HP * half + k
                                out = bank[4 + half][hs, C * k:C * k + C]
                                pe.matmul(out, S[hs, kk_, :], AR[hs, kk_, 1, :], start=True, stop=False)
                                mm = pe.matmul(out, VU[:, kk_, h, :], scores[:, kk_, h, 1, :], start=False, stop=True)
                        mm.then_inc(s["y_pe"], 1)

            def head():
                pe.wait_ge(s["const_ready"], 3)
                low_rank(0)
                key_norm(0)

            def tail():
                n = NCH - 1
                ready(pe, "ysb_out", n - 1, 1, 2)
                pe.matmul(bank[6][:, :], ones_mean[:, :], ysb[:, :, :], start=True, stop=True).then_inc(s["mean_pe"], 1)
                ready(pe, "yc_sq_done", n - 1)
                pe.matmul(bank[7][:, :], ones_mean[:, :], yc_sq[:, :, :], start=True, stop=True).then_inc(s["var_pe"], 1)

            walk(pe, body, head, tail)

        @block.scalar
        def _(act):
            def tanh(n):
                ready(act, "lora_mixed", n)
                if again(n):
                    ready(act, "logits_pe", n - 1)
                act.activation(lora_tanh[:, :], lora[0:DH, :], ACT.Tanh).then_inc(s["tanh_done"], 1)

            def square_keys(n):
                ready(act, "kq_done", n)
                if again(n):
                    ready(act, "norm_pe", n - 1)
                act.activation(kq_sq[:, :, :], kq[:, :, :], ACT.Square).then_inc(s["kq_sq_done"], 1)

            def root_keys(n):
                ready(act, "norm_pe", n)
                if again(n):
                    ready(act, "rnorm_done", n - 1)
                act.activation(k_norm[:, :, :], bank[0][:, :], ACT.Sqrt, bias=omka_eps[:, 0:1]).then_inc(s["norm_done"], 1)

            def sigmoids(n):
                ready(act, "dve_logits", n)
                if again(n):
                    ready(act, "kka_done", n - 1)
                    ready(act, "run_before_done", n - 1)
                    ready(act, "gain", n - 1)
                act.activation(sig[:, :, :, :], logits[:, :, :], ACT.Sigmoid).then_inc(s["sig_done"], 1)

            def decays(n):
                ready(act, "run_before_done", n)
                if again(n):
                    for name in ("a_done", "r_done", "k_done", "b_done", "w_end_done"):
                        ready(act, name, n - 1)
                act.activation(w_now[:, :, :], run[:, :], ACT.Exp, scale=-DECAY_SCALE)
                act.activation(w_inv[:, :, :], run[:, :], ACT.Exp, scale=DECAY_SCALE)
                act.activation(w_before[:, :, :], run_before[:, :], ACT.Exp, scale=-DECAY_SCALE).then_inc(s["exp_done"], 1)

            def square_out(m):
                ready(act, "yc_done", m - 1)
                act.activation(yc_sq[:, :, :], yc[:, :, :], ACT.Square).then_inc(s["yc_sq_done"], 1)

            def root_out(m):
                ready(act, "var_pe", m - 1)
                act.activation(y_std[:, :, :], bank[7][:, :], ACT.Sqrt, bias=t["eps"][:, 1:2]).then_inc(s["std_done"], 1)

            def body(n, prev_out, prep):
                ready(act, "kbt_pe", n)
                for half in range(HALVES):
                    act.copy(KBt[:, HP * half:HP * half + HP, :, :].rearrange("p k h c -> p k (h c)"),
                             bank[2 + half][:, :].rearrange("p (k c) -> p k c", k=HP)).then_inc(s["kbt_out"], 1)
                ready(act, "vt_pe", n)
                for half in range(HALVES):
                    act.copy(VU[0:C, HP * half:HP * half + HP, :, :].rearrange("p k h c -> p k (h c)"),
                             bank[4 + half][0:C, :].rearrange("p (k c) -> p k c", k=HP)).then_inc(s["vt_out"], 1)
                ready(act, "nt_pe", n)
                if again(n):
                    ready(act, "off_done", n - 1, 4, 5)
                act.copy(NT[:, :, :], as_grid(6)).then_inc(s["nt_out"], 1)
                if out_of(n):
                    ready(act, "bonus_pe", n - 1)
                    if prev_out:
                        ready(act, "bonus_v_done", n - 2)
                    act.copy(bonus[:, :, :], as_grid(1)).then_inc(s["bonus_out"], 1)
                for lv in range(len(LEVELS)):
                    for half in range(HALVES):
                        ready(act, "x_pe", n, 2 * lv + half, 10)
                        act.copy(X[:, HP * half:HP * half + HP, :], as_grid(2 + half, HP)).then_inc(s["x_out"], 1)
                    if lv == 0 and prep:
                        tanh(n + 1)
                    if lv == 1:
                        if prev_out:
                            square_out(n - 1)
                        if prep:
                            square_keys(n + 1)
                    if lv == 3:
                        if prev_out:
                            root_out(n - 1)
                        if prep:
                            root_keys(n + 1)
                            sigmoids(n + 1)
                if prep:
                    decays(n + 1)
                ready(act, "lv_pe", n)
                act.copy(LV[:, :, :], as_grid(6)).then_inc(s["lv_out"], 1)
                for half in range(HALVES):
                    ready(act, "u_pe", n, half, 2)
                    act.copy(VU[DH:P, HP * half:HP * half + HP, 0, :],
                             bank[4 + 2 * half][DH:P, 0:HP * C].rearrange("p (k c) -> p k c", k=HP)).then_inc(s["u_out0"], 1)
                if out_of(n):
                    if prev_out:
                        ready(act, "yc_done", n - 2)
                    for half in range(HALVES):
                        ready(act, "y_pe", n - 1, half, 2)
                        act.copy(ysb[:, HP * half:HP * half + HP, :], as_grid(4 + half, HP)).then_inc(s["ysb_out"], 1)

            def head():
                act.wait_ge(s["const_ready"], 3)
                tanh(0)
                square_keys(0)
                root_keys(0)
                sigmoids(0)
                decays(0)

            def tail():
                square_out(NCH - 1)
                root_out(NCH - 1)

            walk(act, body, head, tail)

        @block.vector
        def _(dve):
            def tt(out, a, b, op, name):
                dve.tensor_tensor(out, a, b, op).then_inc(s[name], 1)

            def mix(n):
                dve.wait_ge(s["u_in_ready"], 16 * n + 16)
                if again(n):
                    for name in ("r_done", "kk_done", "k_fin_done", "r_bonus1"):
                        ready(dve, name, n - 1)
                tt(rk_dif[:, :, :], u_in[:, 0:2 * PAIRS, 0:C], u_in[:, 0:2 * PAIRS, 1:], ALU.subtract, "rk_dif")
                ready(dve, "rk_dif", n)
                tt(rk_dif[:, :, :], rk_dif[:, :, :], row(MU, 2 * PAIRS), ALU.mult, "rk_scaled")
                ready(dve, "rk_scaled", n)
                tt(rk[:, :, :], rk_dif[:, :, :], u_in[:, 0:2 * PAIRS, 1:], ALU.add, "rk_mixed")

            def mix_lora(n):
                dve.wait_ge(s["lora_in_ready"], 16 * n + 16)
                if again(n):
                    ready(dve, "logits_pe", n - 1)
                tt(lora_dif[:, :], lora_in[:, 0:C], lora_in[:, 1:], ALU.subtract, "lora_dif")
                ready(dve, "lora_dif", n)
                dve.scalar_tensor_tensor(lora[:, :], lora_dif[:, :], par[:, MU_LORA:MU_LORA + 1], lora_in[:, 1:],
                                         ALU.mult, ALU.add).then_inc(s["lora_mixed"], 1)

            def keys(n):
                ready(dve, "rk_mixed", n)
                if again(n):
                    ready(dve, "kk_done", n - 1)
                    ready(dve, "kq_sq_done", n - 1)
                tt(kq[:, :, :], rk[:, PAIRS:, :], row(K_K), ALU.mult, "kq_done")

            def add_bias(n):
                ready(dve, "logits_pe", n)
                if again(n):
                    ready(dve, "sig_done", n - 1)
                dve.tensor_tensor(logits[:, 0, :].rearrange("p (k c) -> p k c", c=C), as_grid(0), row(W0), ALU.add)
                tt(logits[:, 1, :].rearrange("p (k c) -> p k c", c=C), as_grid(1), row(A0), ALU.add, "dve_logits")

            def running(n):
                ready(dve, "sig_done", n)
                if again(n):
                    ready(dve, "exp_done", n - 1)
                w = sig[:, 0, :, :].rearrange("p k c -> p (k c)")
                dve.tensor_tensor_scan(run[:, :], restart[:, :], w, 0.0, ALU.mult, ALU.add).then_inc(s["run_done"], 1)
                ready(dve, "run_done", n)
                tt(run_before[:, :], run[:, :], w, ALU.subtract, "run_before_done")

            def unit_keys(n):
                ready(dve, "norm_done", n)
                dve.reciprocal(k_rnorm[:, :, :], k_norm[:, :, :]).then_inc(s["rnorm_done"], 1)
                ready(dve, "rnorm_done", n)
                if again(n):
                    ready(dve, "a_done", n - 1)
                    ready(dve, "kka_done", n - 1)
                tt(kk[:, :, :], kq[:, :, :], k_rnorm[:, :, :], ALU.mult, "kk_done")

            def operands(n):
                ready(dve, "exp_done", n)
                if again(n):
                    ready(dve, "s_pe", n - 1, 1, 2)
                    ready(dve, "w_end_done", n - 1)
                tt(AR[:, :, 0, :], kk[:, :, :], w_before[:, :, :], ALU.mult, "a_done")
                ready(dve, "kka_done", n)
                dve.scalar_tensor_tensor(KB[:, :, 1, :], kka[:, :, :], -1.0, w_inv[:, :, :], ALU.mult,
                                         ALU.mult).then_inc(s["b_done"], 1)
                if again(n):
                    ready(dve, "s_done", n - 1)
                dve.tensor_copy(w_end[:, :], w_now[:, :, C - 1]).then_inc(s["w_end_done"], 1)

            def centre(m):
                ready(dve, "mean_pe", m - 1)
                if not isinstance(m, int) or m > 1:
                    ready(dve, "y_n1", m - 2)
                tt(yc[:, :, :], ysb[:, :, :], as_grid(6), ALU.subtract, "yc_done")

            def rstd(m):
                ready(dve, "std_done", m - 1)
                dve.reciprocal(y_rstd[:, :, :], y_std[:, :, :]).then_inc(s["rstd_done"], 1)

            def body(n, prev_out, prep):
                ready(dve, "n_pe", n)
                lower, eye = tri[:, 6, :], tri[:, 7, :]
                for half in range(HALVES):
                    ks = slice(HP * half, HP * half + HP)
                    i_ = dve.tensor_tensor(T2[:, half, 0, :, :], as_grid(7)[:, ks, :],
                                           lower.unsqueeze(1).broadcast_to([P, HP, C]), ALU.mult)
                i_.then_inc(s["t_first"], 1)
                ready(dve, "t_first", n)
                tt(T2[:, :, 0, :, :].rearrange("p a k c -> p a (k c)"), T2[:, :, 0, :, :].rearrange("p a k c -> p a (k c)"),
                   eyes[:, :].unsqueeze(1).broadcast_to([P, HALVES, HP * C]), ALU.add, "t_init")
                for half in range(HALVES):
                    for h in range(2):
                        ready(dve, "st_pe", n, 2 * half + h, 4)
                        dve.tensor_tensor(scores[:, HP * half:HP * half + HP, h, :, :].rearrange("p k a c -> p k (a c)"),
                                          bank[2 + 2 * half + h][:, :].rearrange("p (k c) -> p k c", k=HP),
                                          full[:, :].unsqueeze(1).broadcast_to([P, HP, P]), ALU.mult).then_inc(s["st_out"], 1)
                for lv in range(len(LEVELS)):
                    last = lv == len(LEVELS) - 1
                    for half in range(HALVES):
                        ready(dve, "t_pe", n, 2 * lv + half, 10)
                        a = 1 if last else 0
                        dst = T2[:, half, a:, :, :].rearrange("p a k c -> p (a k c)")
                        tt(dst, dst, bank[4 + half][:, a * HP * C:], ALU.add, "t_out")
                    if lv == 0:
                        if prev_out:
                            centre(n - 1)
                        if prep:
                            mix_lora(n + 1)
                            mix(n + 1)
                            keys(n + 1)
                    if lv == 2 and prep:
                        add_bias(n + 1)
                    if lv == 3:
                        if prep:
                            unit_keys(n + 1)
                            running(n + 1)
                        if prev_out:
                            rstd(n - 1)
                for half in range(HALVES):
                    ks = slice(HP * half, HP * half + HP)
                    ready(dve, "r_pe", n, half, 2)
                    ready(dve, "lv_out", n)
                    tt(R[:, ks, :], as_grid(2 + half, HP), LV[:, ks, :], ALU.add, "r_out")
                for half in range(HALVES):
                    ready(dve, "u_pe", n, half, 2)
                    dve.tensor_copy(VU[DH:P, HP * half:HP * half + HP, 1, :],
                                    bank[5 + 2 * half][DH:P, 0:HP * C].rearrange("p (k c) -> p k c", k=HP)).then_inc(s["u_out1"], 1)
                ready(dve, "s_pe", n, 1, 2)
                for half in range(HALVES):
                    ks = slice(HP * half, HP * half + HP)
                    i_ = dve.tensor_tensor(S_sum[:, ks, :], as_grid(2 + half, HP), S[:, ks, :], ALU.add)
                i_.then_inc(s["s_sum"], 1)
                ready(dve, "s_sum", n)
                if out_of(n):
                    ready(dve, "y_pe", n - 1, 1, 2)
                tt(S[:, :, :], S_sum[:, :, :], w_end[:, :].unsqueeze(2).broadcast_to(grid), ALU.mult, "s_done")
                if prep:
                    operands(n + 1)

            def head():
                dve.memset(S[:, :, :], 0.0)
                dve.memset(omka_eps[:, 0:1], L2_EPS)
                dve.wait_ge(s["const_in"], 96)
                dve.tensor_scalar(ones_mean[:, :], ones_sum[:, :], 1.0 / DH, None, ALU.mult).then_inc(s["const_ready"], 1)
                dve.tensor_scalar(omka[:, :], par[:, K_A:K_A + PAIRS], -1.0, 1.0, ALU.mult, ALU.add).then_inc(s["const_ready"], 1)
                dve.tensor_copy(eyes[:, :].rearrange("p (k c) -> p k c", c=C),
                                tri[:, 7, :].unsqueeze(1).broadcast_to([P, HP, C])).then_inc(s["const_ready"], 1)
                dve.wait_ge(s["const_ready"], 3)
                mix_lora(0)
                mix(0)
                keys(0)
                add_bias(0)
                unit_keys(0)
                running(0)
                operands(0)

            def tail():
                centre(NCH - 1)
                rstd(NCH - 1)

            walk(dve, body, head, tail)

        @block.gpsimd
        def _(pool):
            def tt(out, a, b, op, name):
                pool.tensor_tensor(out, a, b, op).then_inc(s[name], 1)

            def mix_v(n):
                pool.wait_ge(s["v_in_ready"], 16 * n + 16)
                if again(n):
                    ready(pool, "vt_pe", n - 1)
                cur, before = u_in[:, 2 * PAIRS:, 1:], u_in[:, 2 * PAIRS:, 0:C]
                tt(v_dif[:, :, :], before, cur, ALU.subtract, "v_dif")
                ready(pool, "v_dif", n)
                tt(v_dif[:, :, :], v_dif[:, :, :], row(MU + 2 * PAIRS), ALU.mult, "v_scaled")
                ready(pool, "v_scaled", n)
                tt(v_mix[:, :, :], v_dif[:, :, :], cur, ALU.add, "v_mixed")

            def final_keys(n):
                ready(pool, "sig_done", n)
                if again(n):
                    ready(pool, "k_done", n - 1)
                    ready(pool, "b_done", n - 1)
                    ready(pool, "bonus_pe", n - 2) if out_of(n - 1) else None
                a = sig[:, 1, :, :]
                tt(k_gain[:, :, :], a, row(K_A), ALU.mult, "gain")
                ready(pool, "gain", n)
                tt(k_gain[:, :, :], k_gain[:, :, :], omka[:, :].unsqueeze(2).broadcast_to(grid), ALU.add, "gain2")
                ready(pool, "gain2", n)
                tt(k_fin[:, :, :], k_gain[:, :, :], rk[:, PAIRS:, :], ALU.mult, "k_fin_done")
                ready(pool, "k_fin_done", n)
                tt(r_bonus[:, :, :], rk[:, 0:PAIRS, :], row(R_K), ALU.mult, "r_bonus1")
                ready(pool, "r_bonus1", n)
                tt(r_bonus[:, :, :], r_bonus[:, :, :], k_fin[:, :, :], ALU.mult, "r_bonus_done")
                ready(pool, "kk_done", n)
                ready(pool, "r_bonus_done", n)
                tt(kka[:, :, :], a, kk[:, :, :], ALU.mult, "kka_done")

            def operands(n):
                ready(pool, "exp_done", n)
                ready(pool, "kka_done", n)
                if again(n):
                    ready(pool, "s_pe", n - 1, 1, 2)
                tt(KB[:, :, 0, :], k_fin[:, :, :], w_inv[:, :, :], ALU.mult, "k_done")
                ready(pool, "k_done", n)
                if again(n) and out_of(n - 1):
                    ready(pool, "y_pe", n - 2, 1, 2)
                tt(AR[:, :, 1, :], rk[:, 0:PAIRS, :], w_now[:, :, :], ALU.mult, "r_done")

            def normalise(m):
                ready(pool, "rstd_done", m - 1)
                if not isinstance(m, int) or m > 1:
                    pool.wait_ge(s["y_sent"], 16 * (m - 1))
                tt(y_out[:, :, :], yc[:, :, :], y_rstd[:, :, :], ALU.mult, "y_n1")
                ready(pool, "y_n1", m - 1)
                tt(y_out[:, :, :], y_out[:, :, :], row(GN_G), ALU.mult, "y_n2")
                ready(pool, "y_n2", m - 1)
                tt(y_out[:, :, :], y_out[:, :, :], row(GN_B), ALU.add, "y_n3")
                ready(pool, "y_n3", m - 1)
                tt(y_out[:, :, :], y_out[:, :, :], bonus_v[:, :, :], ALU.add, "y_n4")
                ready(pool, "y_n4", m - 1)
                pool.wait_ge(s["gate_in"], 16 * m)
                tt(y_out[:, :, :], y_out[:, :, :], gate[:, :, :], ALU.mult, "y_done")

            def body(n, prev_out, prep):
                ready(pool, "nt_out", n)
                if again(n):
                    ready(pool, "u_pe", n - 1, 1, 2)
                    ready(pool, "r_done", n)
                for half in range(HALVES):
                    ks = slice(HP * half, HP * half + HP)
                    tt(T2[:, half, 1, :, :], NT[:, ks, :], tri[:, 0, :].unsqueeze(1).broadcast_to([P, HP, C]), ALU.mult, "tt_first")
                    ready(pool, "tt_first", n, half, 2)
                for lv in range(len(LEVELS)):
                    tt(off[:, lv, :, :], NT[:, :, :], tri[:, 1 + lv, :].unsqueeze(1).broadcast_to(grid), ALU.mult, "off_done")
                    ready(pool, "off_done", n, lv, len(LEVELS))
                    if lv == 0:
                        tt(T2[:, :, 1, :, :].rearrange("p a k c -> p a (k c)"), T2[:, :, 1, :, :].rearrange("p a k c -> p a (k c)"),
                           eyes[:, :].unsqueeze(1).broadcast_to([P, HALVES, HP * C]), ALU.add, "tt_init")
                        ready(pool, "tt_init", n)
                if prep:
                    final_keys(n + 1)
                if prev_out:
                    normalise(n - 1)
                    ready(pool, "y_done", n - 2)
                if out_of(n):
                    ready(pool, "bonus_out", n - 1)
                    tt(bonus_v[:, :, :], bonus[:, :, :], v_mix[:, :, :], ALU.mult, "bonus_v_done")
                    ready(pool, "bonus_v_done", n - 1)
                if prep:
                    mix_v(n + 1)
                    operands(n + 1)

            def head():
                pool.wait_ge(s["const_ready"], 3)
                final_keys(0)
                mix_v(0)
                ready(pool, "v_mixed", 0)
                operands(0)

            def tail():
                normalise(NCH - 1)

            walk(pool, body, head, tail)



GT = 512
Y_SLOTS, M_SLOTS = 4, 4
OT = 256


def branch_phase(nc, sem, t, io, scratch, w_out_first):
    with ExitStack() as ctx:
        sb = lambda name, shape, dt=F32: ctx.enter_context(nc.sbuf_tensor(name, shape, dt))
        w_hi, w_lo = sb("proj_hi", [P, 2 * KC, D], F32R), sb("proj_lo", [P, 2 * KC, D], F32R)
        w_raw = [sb(f"proj_raw{b}", [P, D]) for b in range(2)]
        y_raw = [sb(f"y_raw{b}", [P, GT]) for b in range(Y_SLOTS)]
        y_hi = [sb(f"y_hi{b}", [P, GT], F32R) for b in range(Y_SLOTS)]
        y_lo = [sb(f"y_lo{b}", [P, GT], F32R) for b in range(Y_SLOTS)]
        gate = [sb(f"merge{b}", [P, GT]) for b in range(M_SLOTS)]
        mixed = sb("mixed", [P, KC, GT])
        bank = [ctx.enter_context(nc.psum_tensor(f"bb{b}", [P, GT], F32)) for b in range(KC)]
        w_in = [sem(f"b_w_in{b}") for b in range(2)]
        y_in = [sem(f"b_y_in{b}") for b in range(Y_SLOTS)]
        gate_in = [sem(f"b_gate_in{b}") for b in range(M_SLOTS)]
        w_high, w_low, y_high, y_low = sem("b_w_high"), sem("b_w_low"), sem("b_y_high"), sem("b_y_low")
        chunk_used, product = sem("b_chunk_used"), sem("b_product")
        gated, mixed_done, mixed_sent = sem("b_gated"), sem("b_mixed"), sem("b_mixed_sent")
        w_out_in = sem("b_w_out_in")
        block = ctx.enter_context(nc.Block())
        CH = 2 * KC

        def walk(eng, body):
            body(0, True)
            with eng.Fori(1, SEQ // GT) as g:
                body(g, False)

        def used(eng, g, c):
            r, k = divmod(c, KC)
            if k == KC - 1:
                eng.wait_ge(product, CH * g + KC * (r + 1))
            else:
                eng.wait_ge(chunk_used, (KC - 1) * (2 * g + r) + k + 1)

        @block.sync
        def _(sp):
            def load_gate(g, e):
                if e >= 0 and (not isinstance(g, int) or e >= M_SLOTS):
                    if M_SLOTS <= e < M_SLOTS + KC:
                        sp.wait_ge(gated, CH * g + e - M_SLOTS + 1)
                    elif e < M_SLOTS:
                        sp.wait_ge(mixed_done, KC * g + e - M_SLOTS + 1)
                    else:
                        sp.wait_ge(mixed_done, KC * g + e - KC - M_SLOTS + 1)
                sp.dma_start(gate[e % M_SLOTS][:, :], scratch["merge"][P * e:P * e + P, bass.ds(GT * g, GT)]).then_inc(
                    gate_in[e % M_SLOTS], 16)

            def load_weights(c):
                if c >= 2:
                    sp.wait_ge(w_low, c - 1)
                sp.dma_start(w_raw[c % 2][:, :], io["w_proj"][P * c:P * c + P, :]).then_inc(w_in[c % 2], 16)

            load_weights(0)
            load_weights(1)

            def body(g, first):
                for c in range(CH):
                    if not first or c >= Y_SLOTS:
                        sp.wait_ge(y_low, CH * g + c - Y_SLOTS + 1)
                    if first and c >= 2:
                        load_weights(c)
                    sp.dma_start(y_raw[c % Y_SLOTS][:, :],
                                 scratch["y"][P * c:P * c + P, bass.ds(GT * g, GT)]).then_inc(y_in[c % Y_SLOTS], 16)
                    if c == 2 and not first:
                        for m in range(4, KC):
                            load_gate(g - 1, KC + m)
                    if c == KC + 2:
                        for m in range(4, KC):
                            load_gate(g, m)
                    if 3 <= c < 7:
                        load_gate(g, c - 3)
                    if KC + 3 <= c < KC + 7:
                        load_gate(g, c - 3)

            walk(sp, body)
            for m in range(4, KC):
                load_gate(SEQ // GT - 1, KC + m)

        @block.scalar
        def _(act):
            def store(g):
                for m in range(KC):
                    act.wait_ge(mixed_done, KC * g + m + 1)
                    act.dma_start(scratch["mixed"][P * m:P * m + P, bass.ds(GT * g, GT)], mixed[:, m, :]).then_inc(mixed_sent, 16)

            def body(g, first):
                for c in range(CH):
                    if first:
                        act.wait_ge(w_in[c % 2], 16 * (c // 2) + 16)
                        act.copy(w_hi[:, c, :], w_raw[c % 2][:, :]).then_inc(w_high, 1)
                    if not first or c >= Y_SLOTS:
                        used(act, g, c - Y_SLOTS)
                    act.wait_ge(y_in[c % Y_SLOTS], 16 * (CH // Y_SLOTS * g + c // Y_SLOTS) + 16)
                    act.copy(y_hi[c % Y_SLOTS][:, :], y_raw[c % Y_SLOTS][:, :]).then_inc(y_high, 1)
                    if c == 4 and not first:
                        store(g - 1)
                if first:
                    act.dma_start(w_out_first[:, :, :], io["w_out"][0:D // 2, :].rearrange("(k p) c -> p k c", p=P)).then_inc(w_out_in, 16)

            walk(act, body)
            store(SEQ // GT - 1)
            act.wait_ge(w_out_in, 16)
            act.wait_ge(mixed_sent, 16 * KC * (SEQ // GT))

        @block.tensor
        def _(pe):
            def body(g, first):
                for c in range(CH):
                    if first:
                        pe.wait_ge(w_low, c + 1)
                    pe.wait_ge(y_low, CH * g + c + 1)
                    k = c % KC
                    for m in range(KC):
                        if k == 0 and not (first and c == 0):
                            pe.wait_ge(gated, CH * g + c - KC + m + 1)
                        cols = slice(P * m, P * m + P)
                        pe.matmul(bank[m][:, :], w_hi[:, c, cols], y_hi[c % Y_SLOTS][:, :], start=k == 0, stop=False)
                        pe.matmul(bank[m][:, :], w_hi[:, c, cols], y_lo[c % Y_SLOTS][:, :], start=False, stop=False)
                        mm = pe.matmul(bank[m][:, :], w_lo[:, c, cols], y_hi[c % Y_SLOTS][:, :], start=False,
                                       stop=k == KC - 1)
                        if k == KC - 1:
                            mm.then_inc(product, 1)
                        elif m == KC - 1:
                            mm.then_inc(chunk_used, 1)

            walk(pe, body)

        @block.vector
        def _(dve):
            def mix(g, r):
                if r == 0 and not isinstance(g, int):
                    dve.wait_ge(mixed_sent, 16 * KC * g)
                for m in range(KC):
                    e = KC * r + m
                    dve.wait_ge(product, CH * g + e + 1)
                    dve.wait_ge(gate_in[e % M_SLOTS], 16 * (CH // M_SLOTS * g + e // M_SLOTS) + 16)
                    dst = gate[e % M_SLOTS][:, :] if r else mixed[:, m, :]
                    dve.tensor_tensor(dst, bank[m][:, :], gate[e % M_SLOTS][:, :], ALU.mult).then_inc(gated, 1)

            def body(g, first):
                for c in range(CH):
                    if first:
                        dve.wait_ge(w_high, c + 1)
                        dve.tensor_tensor(w_lo[:, c, :], w_raw[c % 2][:, :], w_hi[:, c, :].bitcast(F32),
                                          ALU.subtract).then_inc(w_low, 1)
                    dve.wait_ge(y_high, CH * g + c + 1)
                    dve.tensor_tensor(y_lo[c % Y_SLOTS][:, :], y_raw[c % Y_SLOTS][:, :], y_hi[c % Y_SLOTS][:, :].bitcast(F32), ALU.subtract).then_inc(y_low, 1)
                    if c == 1 and not first:
                        mix(g - 1, 1)
                    if c == KC + 1:
                        mix(g, 0)

            walk(dve, body)
            mix(SEQ // GT - 1, 1)

        @block.gpsimd
        def _(pool):
            with pool.Fori(0, SEQ // GT) as g:
                for m in range(KC):
                    pool.wait_ge(gated, CH * g + KC + m + 1)
                    pool.tensor_tensor(mixed[:, m, :], mixed[:, m, :], gate[m % M_SLOTS][:, :], ALU.add).then_inc(mixed_done, 1)


def output_phase(nc, sem, t, io, out, scratch, w_first):
    with ExitStack() as ctx:
        sb = lambda name, shape, dt=F32: ctx.enter_context(nc.sbuf_tensor(name, shape, dt))
        w_second = sb("w_out_second", [P, KC // 2, D])
        w_hi, w_lo = sb("w_out_hi", [P, KC, D], F32R), sb("w_out_lo", [P, KC, D], F32R)
        m_raw = [sb(f"m_raw{b}", [P, KC, OT]) for b in range(2)]
        m_hi = [sb(f"m_hi{b}", [P, KC, OT], F32R) for b in range(2)]
        m_lo = [sb(f"m_lo{b}", [P, KC, OT], F32R) for b in range(2)]
        x = [sb(f"x_res{b}", [P, D]) for b in range(2)]
        normed = [sb(f"o_normed{b}", [P, D]) for b in range(2)]
        result = [sb(f"o_result{b}", [P, D]) for b in range(2)]
        squares = sb("o_squares", [P, D])
        post_g = sb("post_g", [P, D])
        ssum = [sb(f"o_ssum{b}", [P, 1]) for b in range(2)]
        std = [sb(f"o_std{b}", [P, 1]) for b in range(2)]
        rinv = [sb(f"o_rinv{b}", [P, 1]) for b in range(2)]
        acc = [ctx.enter_context(nc.psum_tensor(f"oo{b}", [P, D], F32)) for b in range(2)]
        g_in, w_high, w_low = sem("o_g_in"), sem("o_w_high"), sem("o_w_low")
        w_in = sem("o_w_in")
        m_in = [sem(f"o_m_in{b}") for b in range(2)]
        x_in = [sem(f"o_x_in{b}") for b in range(2)]
        sent = [sem(f"o_sent{b}") for b in range(2)]
        m_high, m_low, product = sem("o_m_high"), sem("o_m_low"), sem("o_product")
        summed, rooted, inverted, scaled, added = sem("o_summed"), sem("o_rooted"), sem("o_inverted"), sem("o_scaled"), sem("o_added")
        block = ctx.enter_context(nc.Block())
        TILES = SEQ // P
        GROUPS_O = SEQ // OT

        def raw(k):
            return w_first[:, k, :] if k < KC // 2 else w_second[:, k - KC // 2, :]

        @block.sync
        def _(sp):
            def load(j, b):
                sp.dma_start(m_raw[b][:, :, :], scratch["mixed"][:, bass.ds(OT * j, OT)].rearrange(
                    "(k p) c -> p k c", p=P)).then_inc(m_in[b], 16)

            load(0, 0)
            sp.dma_start(w_second[:, :, :], io["w_out"][D // 2:, :].rearrange("(k p) c -> p k c", p=P)).then_inc(w_in, 16)
            sp.dma_start(x[0][:, :], io["x"][0:P, :]).then_inc(x_in[0], 16)
            sp.dma_start(post_g[:, :], io["post_norm_g"].broadcast_to([P, D])).then_inc(g_in, 16)
            load(1, 1)
            sp.dma_start(x[1][:, :], io["x"][P:2 * P, :]).then_inc(x_in[1], 16)
            with sp.Fori(0, GROUPS_O // 2 - 1) as i:
                for b in range(2):
                    for u in range(2):
                        sp.wait_ge(added, 4 * i + 2 * b + u + 1)
                        sp.dma_start(x[u][:, :], io["x"][bass.ds(P * (4 * i + 2 * b + u + 2), P), :]).then_inc(x_in[u], 16)
                    load(2 * i + b + 2, b)
            for u in range(2):
                sp.wait_ge(added, TILES - 4 + u + 1)
                sp.dma_start(x[u][:, :], io["x"][P * (TILES - 2 + u):P * (TILES - 1 + u), :]).then_inc(x_in[u], 16)

        @block.scalar
        def _(act):
            def split(j, b):
                act.wait_ge(m_in[b], 16 * ((j - b) // 2) + 16)
                act.copy(m_hi[b][:, :, :], m_raw[b][:, :, :]).then_inc(m_high, 1)

            def norm(n, u):
                act.wait_ge(product, n + 1)
                act.activation(squares[:, :], acc[u][:, :], ACT.Square, accum_out=ssum[u][:, :]).then_inc(summed, 1)
                act.wait_ge(summed, n + 1)
                act.activation(std[u][:, :], ssum[u][:, :], ACT.Sqrt, scale=1.0 / D, bias=t["eps"][:, 0:1]).then_inc(rooted, 1)

            def store(n, u):
                act.wait_ge(added, n + 1)
                act.dma_start(out[bass.ds(P * n, P), :], result[u][:, :]).then_inc(sent[u], 16)

            for u in range(2):
                act.sem_inc(sent[u], 16)
            split(0, 0)
            for k in range(KC):
                if k == KC // 2:
                    act.wait_ge(w_in, 16)
                act.copy(w_hi[:, k, :], raw(k)).then_inc(w_high, 1)
            norm(0, 0)
            split(1, 1)
            norm(1, 1)
            store(0, 0)
            with act.Fori(0, GROUPS_O // 2 - 1) as i:
                for b in range(2):
                    n = 4 * i + 2 * b + 2
                    norm(n, 0)
                    store(n - 1, 1)
                    split(2 * i + b + 2, b)
                    norm(n + 1, 1)
                    store(n, 0)
            n = TILES - 2
            norm(n, 0)
            store(n - 1, 1)
            norm(n + 1, 1)
            store(n, 0)
            store(n + 1, 1)
            for u in range(2):
                act.wait_ge(sent[u], 16 * (TILES // 2) + 16)

        @block.tensor
        def _(pe):
            pe.wait_ge(w_low, KC)
            with pe.Fori(0, GROUPS_O // 2) as i:
                for b in range(2):
                    pe.wait_ge(m_low, 2 * i + b + 1)
                    for u in range(2):
                        n = 4 * i + 2 * b + u
                        pe.wait_ge(scaled, n + 1)
                        tok = slice(P * u, P * u + P)
                        for half in range(2):
                            cols = slice(512 * half, 512 * half + 512)
                            for k in range(KC):
                                dst = acc[u][:, cols]
                                pe.matmul(dst, m_hi[b][:, k, tok], w_hi[:, k, cols], start=k == 0, stop=False)
                                pe.matmul(dst, m_hi[b][:, k, tok], w_lo[:, k, cols], start=False, stop=False)
                                mm = pe.matmul(dst, m_lo[b][:, k, tok], w_hi[:, k, cols], start=False, stop=k == KC - 1)
                        mm.then_inc(product, 1)

        @block.vector
        def _(dve):
            def split(j, b):
                dve.wait_ge(m_high, j + 1)
                dve.tensor_tensor(m_lo[b][:, :, :], m_raw[b][:, :, :], m_hi[b][:, :, :].bitcast(F32),
                                  ALU.subtract).then_inc(m_low, 1)

            def norm(n, u):
                dve.wait_ge(rooted, n + 1)
                dve.reciprocal(rinv[u][:, :], std[u][:, :]).then_inc(inverted, 1)
                dve.wait_ge(inverted, n + 1)
                if not isinstance(n, int) or n >= 2:
                    dve.wait_ge(added, n - 1)
                dve.scalar_tensor_tensor(normed[u][:, :], acc[u][:, :], rinv[u][:, 0:1], post_g[:, :], ALU.mult,
                                         ALU.mult).then_inc(scaled, 1)

            split(0, 0)
            for k in range(KC):
                dve.wait_ge(w_high, k + 1)
                dve.tensor_tensor(w_lo[:, k, :], raw(k), w_hi[:, k, :].bitcast(F32),
                                  ALU.subtract).then_inc(w_low, 1)
            dve.wait_ge(g_in, 16)
            dve.sem_inc(scaled, 2)
            norm(0, 0)
            split(1, 1)
            norm(1, 1)
            with dve.Fori(0, GROUPS_O // 2 - 1) as i:
                for b in range(2):
                    n = 4 * i + 2 * b + 2
                    norm(n, 0)
                    split(2 * i + b + 2, b)
                    norm(n + 1, 1)
            norm(TILES - 2, 0)
            norm(TILES - 1, 1)

        @block.gpsimd
        def _(pool):
            with pool.Fori(0, TILES // 2) as i:
                for u in range(2):
                    n = 2 * i + u
                    pool.wait_ge(scaled, n + 3)
                    pool.wait_ge(x_in[u], 16 * i + 16)
                    pool.wait_ge(sent[u], 16 * i + 16)
                    pool.tensor_tensor(result[u][:, :], normed[u][:, :], x[u][:, :], ALU.add).then_inc(added, 1)

def program(nc, io, out):
    with ExitStack() as ctx:
        taken = []

        def sem(name):
            taken.append(nc.alloc_semaphore(name))
            return taken[-1]

        dram = lambda name, shape: nc.dram_tensor("scr_" + name, shape, F32, kind="Internal").ap()
        scratch = {
            "u": dram("u", (3 * D + P, 1 + TOK)),
            "qk": dram("qk", (2 * D, TOK)),
            "v_sb": dram("v_sb", (TOK, D)),
            "gates": dram("gates", (2 * D, SEQ)),
            "merge": dram("merge", (2 * D, SEQ)),
            "y": dram("y", (2 * D, SEQ)),
            "mixed": dram("mixed", (D, SEQ)),
        }
        sb = lambda name, shape, dt=F32: ctx.enter_context(nc.sbuf_tensor(name, shape, dt))
        t = {"identity": sb("t_identity", [P, P]), "pre_g": sb("t_pre_g", [P, KC]), "eps": sb("t_eps", [P, 2])}
        with ExitStack() as held:
            for part in ("hn_hi", "hn_lo"):
                t[part] = held.enter_context(nc.sbuf_tensor(part, [P, KC, TOK], F32R))
            norm_phase(nc, sem, t, io)
            project_phase(nc, sem, t, io, scratch)
        attention_phase(nc, sem, t, io, scratch)
        rwkv_phase(nc, sem, t, io, scratch)
        nc.clear_and_free_semaphores(taken)
        nc.all_engine_barrier()
        w_out_first = sb("w_out_first", [P, KC // 2, D])
        branch_phase(nc, sem, t, io, scratch, w_out_first)
        output_phase(nc, sem, t, io, out, scratch, w_out_first)


def kernel(x, meta_tokens, pre_norm_g, post_norm_g, w_in, rwkv_mu, rwkv_w0, rwkv_w_up, rwkv_a0, rwkv_a_up,
           rwkv_k_k, rwkv_k_a, rwkv_r_k, rwkv_gn_g, rwkv_gn_b, w_proj_rwkv, w_proj_sb, w_out):
    import numpy as np
    import concourse.bacc as bacc
    from concourse.bass_utils import run_bass_kernel_spmd

    def channels(a):
        return a.reshape(-1, P).T

    shift, lora = 3 * D, P
    main = np.concatenate([w_in[0][:, :shift], w_in[0][:, shift + lora:]], axis=1)
    w_main = main.reshape(KC, P, -1, WB).transpose(2, 1, 0, 3).reshape(-1, P, KC * WB)
    w_lora = np.zeros((KC, P, WB), w_in.dtype)
    w_lora[:, :, :lora] = w_in[0][:, shift:shift + lora].reshape(KC, P, lora)
    params = np.concatenate([channels(rwkv_mu[0])] + [channels(a[0]) for a in (
        rwkv_w0, rwkv_a0, rwkv_k_k, rwkv_k_a, rwkv_r_k, rwkv_gn_g, rwkv_gn_b)], axis=1)

    j, i = np.arange(CHUNK)[:, None], np.arange(CHUNK)[None, :]
    joins = [((j // (2 * s) == i // (2 * s)) & (j // s < i // s)) for s in [1] + LEVELS]
    tri = np.stack(joins + [joins[0].T, j == i], axis=1).reshape(CHUNK, -1)
    before, upto = j < i, j <= i
    full = np.block([[before, upto], [np.zeros_like(before), upto]])
    restart = np.ones((P, PAIRS, CHUNK))
    restart[:, :, 0] = 0
    q, k = np.arange(P)[:, None], np.arange(P)[None, :]
    f32 = lambda a: np.ascontiguousarray(np.asarray(a, np.float32))
    given = {
        "x": x[0], "meta_tokens": meta_tokens, "pre_norm_g": channels(pre_norm_g[0]), "post_norm_g": post_norm_g,
        "w_main": w_main, "w_lora": w_lora.transpose(1, 0, 2).reshape(P, -1), "params": params,
        "up": np.concatenate([rwkv_w_up[0], rwkv_a_up[0]], axis=0),
        "w_proj": np.concatenate([w_proj_rwkv[0], w_proj_sb[0]], axis=0), "w_out": w_out[0],
    }
    constants = {
        "identity": f32(np.eye(P)), "hidden": f32(np.where(k >= q, HIDDEN, 0)), "last_row": f32(q != P - 1),
        "tri": f32(np.concatenate([tri, tri], axis=0)), "full": f32(full),
        "ones_sum": f32(np.kron(np.eye(2), np.ones((DH, DH)))), "restart": f32(restart.reshape(P, -1)),
    }
    nc = bacc.Bacc("TRN2", target_bir_lowering=False, num_devices=1)
    arrays, io = {}, {}
    for name, a in {**given, **constants}.items():
        arrays["in_" + name] = np.ascontiguousarray(a)
        io[name] = nc.dram_tensor("in_" + name, a.shape, mybir.dt.from_np(a.dtype), kind="ExternalInput").ap()
    out = nc.dram_tensor("out", (SEQ, D), F32, kind="ExternalOutput").ap()
    program(nc, io, out)
    result = run_bass_kernel_spmd(nc, [arrays], core_ids=[0])
    return result.results[0]["out"].reshape(1, SEQ, D)
```

```python
from contextlib import ExitStack

import concourse.bass as bass
from concourse import mybir

ALU = mybir.AluOpType
ACT = mybir.ActivationFunctionType
F32 = mybir.dt.float32
F32R = mybir.dt.float32r

P = 128
D = 1024
SEQ = 2048
META = 16
HEADS = 16
DH = 64
PAIRS = HEADS // 2
KC = D // P
CHUNK = 64
PAD = CHUNK - META
TOK = PAD + META + SEQ
NCH = TOK // CHUNK
RMS_EPS = 1e-6
GN_EPS = 64e-5
L2_EPS = 1e-12
DECAY_SCALE = 0.6065306597126334

WB = 256
GS = [424, 424, 424, 424, 416]
GR = [512] * 4
STREAM, SILU, SIGMOID, TOKENS = range(4)
SEGMENTS = [
    (0, 12, STREAM, "u", 0),
    (16, 8, STREAM, "qk", 0),
    (12, 4, SILU, "gates", 0),
    (28, 4, SILU, "gates", D),
    (32, 8, SIGMOID, "merge", 0),
    (24, 4, TOKENS, "v_sb", 0),
]


def starts(sizes, at):
    out = []
    for s in sizes:
        out.append((at, s))
        at += s
    return out


def norm_phase(nc, sem, t, io):
    with ExitStack() as ctx:
        sb = lambda name, shape, dt=F32: ctx.enter_context(nc.sbuf_tensor(name, shape, dt))
        x = [sb(f"x{b}", [P, D]) for b in range(2)]
        hn = [sb(f"hn{b}", [P, D]) for b in range(2)]
        gained = [sb(f"gained{b}", [P, KC, P]) for b in range(2)]
        ssum = [sb(f"ssum{b}", [P, 1]) for b in range(2)]
        std = [sb(f"std{b}", [P, 1]) for b in range(2)]
        rinv = [sb(f"rinv{b}", [P, 1]) for b in range(2)]
        pt = [ctx.enter_context(nc.psum_tensor(f"pt{b}", [P, KC, P], F32)) for b in range(2)]
        const_in, zeroed = sem("n_const_in"), sem("n_zeroed")
        x_in = [sem(f"n_x_in{b}") for b in range(2)]
        summed, rooted, inverted, normed = sem("n_summed"), sem("n_rooted"), sem("n_inverted"), sem("n_normed")
        turned, gain_done, high_done, low_done = sem("n_turned"), sem("n_gain"), sem("n_high"), sem("n_low")
        block = ctx.enter_context(nc.Block())

        LAST = SEQ // P

        def place(n):
            return 0 if isinstance(n, int) and n == 0 else CHUNK + P * (n - 1)

        def tiles(eng, norm, split):
            norm(0, 1, CHUNK)
            norm(1, 0, P)
            split(0, 1, CHUNK, 0)
            with eng.Fori(1, LAST // 2) as i:
                for b in range(2):
                    n = 2 * i + b
                    norm(n, 1 - b, P)
                    split(n - 1, b, P, place(n - 1))
            norm(LAST, 1, P)
            split(LAST - 1, 0, P, place(LAST - 1))
            split(LAST, 1, P, place(LAST))

        def moves(n):
            return not isinstance(n, int) or n > 1

        @block.sync
        def _(sp):
            sp.dma_start(t["identity"][:, :], io["identity"]).then_inc(const_in, 16)
            sp.dma_start(t["pre_g"][:, :], io["pre_norm_g"]).then_inc(const_in, 16)
            sp.wait_ge(zeroed, 1)
            sp.dma_start(x[1][PAD:CHUNK, :], io["meta_tokens"]).then_inc(x_in[1], 16)
            sp.dma_start(x[0][:, :], io["x"][0:P, :]).then_inc(x_in[0], 16)
            sp.wait_ge(normed, 1)
            sp.dma_start(x[1][:, :], io["x"][P:2 * P, :]).then_inc(x_in[1], 16)
            with sp.Fori(1, SEQ // P // 2) as i:
                for b in range(2):
                    sp.wait_ge(normed, 2 * i + b)
                    sp.dma_start(x[b][:, :], io["x"][bass.ds(P * (2 * i + b), P), :]).then_inc(x_in[b], 16)

        @block.scalar
        def _(act):
            def norm(n, b, m):
                act.wait_ge(x_in[b], 16 * (n // 2) + 16)
                if moves(n):
                    act.wait_ge(turned, n - 1)
                act.activation(hn[b][0:m, :], x[b][0:m, :], ACT.Square, accum_out=ssum[b][0:m, :]).then_inc(summed, 1)
                act.wait_ge(summed, n + 1)
                act.activation(std[b][0:m, :], ssum[b][0:m, :], ACT.Sqrt, scale=1.0 / D,
                               bias=t["eps"][0:m, 0:1]).then_inc(rooted, 1)

            def split(n, b, m, tok):
                act.wait_ge(gain_done, n + 1)
                act.copy(t["hn_hi"][:, :, bass.ds(tok, m)], gained[b][:, :, 0:m]).then_inc(high_done, 1)

            act.wait_ge(zeroed, 3)
            tiles(act, norm, split)

        @block.tensor
        def _(pe):
            def turn(n, b, m):
                pe.wait_ge(normed, n + 1)
                if moves(n):
                    pe.wait_ge(gain_done, n - 1)
                for k in range(KC):
                    mm = pe.transpose(pt[b][:, k, 0:m], hn[b][0:m, k * P:(k + 1) * P], t["identity"][0:m, 0:m])
                mm.then_inc(turned, 1)

            pe.wait_ge(const_in, 32)
            tiles(pe, turn, lambda *tile: None)

        @block.vector
        def _(dve):
            dve.memset(x[1][0:CHUNK, :], 0.0).then_inc(zeroed, 1)
            dve.memset(t["eps"][:, 0:1], RMS_EPS).then_inc(zeroed, 1)
            dve.memset(t["eps"][:, 1:2], GN_EPS).then_inc(zeroed, 1)
            dve.wait_ge(const_in, 32)

            def norm(n, b, m):
                dve.wait_ge(rooted, n + 1)
                dve.reciprocal(rinv[b][0:m, :], std[b][0:m, :]).then_inc(inverted, 1)
                dve.wait_ge(inverted, n + 1)
                dve.tensor_scalar(hn[b][0:m, :], x[b][0:m, :], rinv[b][0:m, 0:1], None, ALU.mult).then_inc(normed, 1)

            def split(n, b, m, tok):
                dve.wait_ge(turned, n + 1)
                if moves(n):
                    dve.wait_ge(low_done, n - 1)
                for half in range(2):
                    ks = slice(4 * half, 4 * half + 4)
                    g = dve.tensor_tensor(gained[b][:, ks, 0:m], pt[b][:, ks, 0:m],
                                          t["pre_g"][:, ks].unsqueeze(2).broadcast_to([P, 4, m]), ALU.mult)
                g.then_inc(gain_done, 1)

            tiles(dve, norm, split)

        @block.gpsimd
        def _(pool):
            def split(n, b, m, tok):
                pool.wait_ge(high_done, n + 1)
                pool.tensor_tensor(t["hn_lo"][:, :, bass.ds(tok, m)], gained[b][:, :, 0:m],
                                   t["hn_hi"][:, :, bass.ds(tok, m)].bitcast(F32), ALU.subtract).then_inc(low_done, 1)

            tiles(pool, lambda *tile: None, split)


def project_phase(nc, sem, t, io, scratch):
    with ExitStack() as ctx:
        sb = lambda name, shape, dt=F32: ctx.enter_context(nc.sbuf_tensor(name, shape, dt))
        raw = [sb(f"w_raw{b}", [P, KC, WB]) for b in range(2)]
        hi = [sb(f"w_hi{b}", [P, KC, WB], F32R) for b in range(2)]
        lo = [sb(f"w_lo{b}", [P, KC, WB], F32R) for b in range(2)]
        stage = [sb(f"stage{b}", [P, 512]) for b in range(2)]
        zero = sb("zero_col", [P, 3 * KC + 1])
        bank = [ctx.enter_context(nc.psum_tensor(f"pp{b}", [P, 512], F32)) for b in range(2)]
        w_in = [sem(f"p_w_in{b}") for b in range(2)]
        high, low = sem("p_high"), sem("p_low")
        product, staged = sem("p_product"), sem("p_staged")
        sent = [sem(f"p_sent{b}") for b in range(2)]
        zeroed, zeros_sent = sem("p_zeroed"), sem("p_zeros_sent")
        block = ctx.enter_context(nc.Block())

        def groups(kind):
            if kind == TOKENS:
                return [(None, 0, CHUNK)] + [(None, CHUNK + P * k, P) for k in range(SEQ // P)]
            sizes = starts(GS, 0) if kind == STREAM else starts(GR, CHUNK)
            return [(m, at, n) for m in range(WB // P) for at, n in sizes]

        def walk(eng, step):
            step(0, 0, 0, STREAM, None, None)
            n0, q0 = 1, len(GS)
            for seg in SEGMENTS:
                first, count, kind, _, _ = seg
                per = len(groups(kind))
                with eng.Fori(0, count // 2) as i:
                    for u in range(2):
                        step(n0 + u + 2 * i, (n0 + u) % 2, (q0 + u * per, i * 2 * per), kind, 2 * i + u, seg)
                n0 += count
                q0 += count * per

        def number(q, g):
            if isinstance(q, int):
                return q + g, (q + g) % 2, (q + g) // 2
            base, moving = q
            return base + g + moving, (base + g) % 2, (base + g) // 2 + moving // 2

        def of_block(kind, n):
            return groups(STREAM)[:len(GS)] if isinstance(n, int) else groups(kind)

        @block.sync
        def _(sp):
            def step(n, b, q, kind, blk, seg):
                src = io["w_lora"] if seg is None else io["w_main"][bass.ds(seg[0] + blk, 1)].rearrange(
                    "o p k -> (o p) k")
                if not isinstance(n, int):
                    sp.wait_ge(low, n)
                sp.dma_start(raw[b][:, :, :], src.rearrange("p (k c) -> p k c", k=KC)).then_inc(w_in[b], 16)

            walk(sp, step)

        @block.vector
        def _(dve):
            dve.memset(zero[:, :], 0.0).then_inc(zeroed, 1)
            dve.sem_inc(low, 1)

            def step(n, b, q, kind, blk, seg):
                uses = 1 if isinstance(n, int) else (n + 2 - b) // 2
                dve.wait_ge(w_in[b], 16 * uses)
                if not isinstance(n, int):
                    margin = min(len(GS), len(groups(kind))) - 1
                    dve.wait_ge(product, q[0] + q[1] - margin)
                dve.tensor_copy(hi[b][:, :, :], raw[b][:, :, :]).then_inc(high, 1)
                dve.wait_ge(high, n + 1)
                dve.tensor_tensor(lo[b][:, :, :], raw[b][:, :, :], hi[b][:, :, :].bitcast(F32),
                                  ALU.subtract).then_inc(low, 1)

            walk(dve, step)

        @block.tensor
        def _(pe):
            def step(n, b, q, kind, blk, seg):
                pe.wait_ge(low, n + 2)
                for g, (m, at, size) in enumerate(of_block(kind, n)):
                    num, slot, uses = number(q, g)
                    if not isinstance(num, int):
                        pe.wait_ge(staged, num - 1)
                    elif num >= 2:
                        pe.wait_ge(staged, num - 1)
                    passes = [(hi, "hn_hi"), (hi, "hn_lo"), (lo, "hn_hi")]
                    for k in range(KC):
                        for w, h in passes:
                            acts = t[h][:, k, at:at + size]
                            if m is None:
                                out, lhs, rhs = bank[slot][0:size, 0:WB], acts, w[b][:, k, :]
                            else:
                                out, lhs, rhs = bank[slot][:, 0:size], w[b][:, k, m * P:(m + 1) * P], acts
                            first = k == 0 and (w, h) == passes[0]
                            last = k == KC - 1 and (w, h) == passes[2]
                            mm = pe.matmul(out, lhs, rhs, start=first, stop=last)
                    mm.then_inc(product, 1)

            walk(pe, step)

        @block.scalar
        def _(act):
            act.wait_ge(zeroed, 1)
            act.dma_start(scratch["u"][:, 0:1].rearrange("(k p) c -> p k c", p=P), zero[:, :].unsqueeze(2),
                          allow_slow_non_contiguous=True).then_inc(zeros_sent, 16)

            def step(n, b, q, kind, blk, seg):
                for g, (m, at, size) in enumerate(of_block(kind, n)):
                    num, slot, uses = number(q, g)
                    act.wait_ge(product, num + 1)
                    if not isinstance(num, int) or num >= 2:
                        act.wait_ge(sent[slot], 16 * uses)
                    rows, cols = (size, WB) if m is None else (P, size)
                    func = {STREAM: ACT.Copy, TOKENS: ACT.Copy, SILU: ACT.Silu, SIGMOID: ACT.Sigmoid}[kind]
                    act.activation(stage[slot][0:rows, 0:cols], bank[slot][0:rows, 0:cols], func).then_inc(staged, 1)
                    act.wait_ge(staged, num + 1)
                    if seg is None:
                        dst = scratch["u"][3 * D:3 * D + P, 1 + at:1 + at + size]
                    elif m is None:
                        dst = scratch["v_sb"][at:at + size, bass.ds(blk * WB, WB)]
                    else:
                        off = {"u": 1 + at, "qk": at}.get(seg[3], at - CHUNK)
                        dst = scratch[seg[3]][bass.ds(blk * WB + seg[4] + m * P, P), off:off + size]
                    act.dma_start(dst, stage[slot][0:rows, 0:cols]).then_inc(sent[slot], 16)

            walk(act, step)
            total = len(GS) + sum(c * len(groups(k)) for _, c, k, _, _ in SEGMENTS)
            act.wait_ge(zeros_sent, 16)
            for slot in range(2):
                act.wait_ge(sent[slot], 16 * ((total + 1 - slot) // 2))


QT = SEQ // P
GROUP = 4
GROUPS = QT // GROUP
HIDDEN = -1e30


def keys_of(qt):
    return META + P * (qt + 1)


def pieces_of(qt):
    out, end = [], keys_of(qt)
    while end:
        size = min(512, end)
        out.append((end - size, size))
        end -= size
    return out


def rank(g):
    return min(g, 2 * GROUPS - 1 - g)


def merged(slow, fast):
    out, a, b = [], 0, 0
    while a < len(slow) or b < len(fast):
        if b >= len(fast) or (a < len(slow) and (a + 1) * len(fast) <= b * len(slow)):
            out.append(slow[a])
            a += 1
        else:
            out.append(fast[b])
            b += 1
    return out


def attention_schedule():
    logits, values = [], []
    nl = nv = 0
    for g in range(2 * GROUPS):
        rows = []
        for qt in range(GROUP * rank(g), GROUP * (rank(g) + 1)):
            for k0, size in pieces_of(qt):
                rows.append(("logits", g, qt, k0, size, nl))
                nl += 1
        logits.append(rows)
        rows = []
        for kt in range(-1, GROUP * (rank(g) + 1)):
            rows.append(("values", g, kt, nv))
            nv += 1
        values.append(rows)
    order = list(logits[0])
    for g in range(2 * GROUPS):
        order += merged(values[g], logits[g + 1] if g + 1 < 2 * GROUPS else [])
    return order, nl, nv

def finishing(order, last_values, lag):
    out, steps, due = [], 0, []
    for e in order:
        out.append(e)
        if e[0] == "values":
            steps += 1
            while due and steps >= due[0][1]:
                out.append(("sum", due.pop(0)[0]))
            if e[3] == last_values[e[1]]:
                due.append((e[1], steps + lag + 1))
    return out + [("sum", g) for g, _ in due]



def attention_phase(nc, sem, t, io, scratch):
    order, n_logits, n_values = attention_schedule()
    LAG, ZB, TB, KB = 3, 2, 4, 4
    assert n_logits % ZB == n_logits % KB == n_values % TB == 0
    last_logits = {e[1]: e[5] for e in order if e[0] == "logits"}
    last_values = {e[1]: e[3] for e in order if e[0] == "values"}
    with ExitStack() as ctx:
        sb = lambda name, shape, dt=F32: ctx.enter_context(nc.sbuf_tensor(name, shape, dt))
        ps = lambda name, shape: ctx.enter_context(nc.psum_tensor(name, shape, F32))
        q_raw, k_raw = sb("q_raw", [P, SEQ]), sb("k_raw", [P, META + SEQ])
        v_now, v_before = sb("v_now", [P, 1 + QT, DH]), sb("v_before", [P, 1 + QT, DH])
        v_diff = sb("v_diff", [P, 1 + QT, DH])
        q_parts = [sb(f"q_parts{b}", [P, SEQ], F32R) for b in range(2)]
        k_high = [sb(f"k_high{b}", [P, META + SEQ], F32R) for b in range(2)]
        k_low = [sb(f"k_low{b}", [P, META + SEQ], F32R) for b in range(2)]
        dv = [sb(f"dv{b}", [P, 1 + QT, 2, DH], F32R) for b in range(2)]
        dv_diag = [sb(f"dv_diag{b}", [P, QT, 2, DH], F32R) for b in range(2)]
        longest = sum(keys_of(qt) for qt in range(QT - GROUP, QT))
        kept = [sb(f"kept{b}", [P, longest]) for b in range(2)]
        keep = [sb(f"keep{b}", [P, 512]) for b in range(KB)]
        w_high = [sb(f"w_high{b}", [P, 512], F32R) for b in range(TB)]
        w_low = [sb(f"w_low{b}", [P, 512], F32R) for b in range(TB)]
        low_half = sb("low_half", [DH, 512])
        total = sb("total", [DH, 512])
        gate = [sb(f"gate{b}", [DH, 512]) for b in range(2)]
        y = [sb(f"y_sb{b}", [DH, 512]) for b in range(2)]
        hidden, eye = sb("hidden", [P, P], F32R), sb("eye_r", [P, P], F32R)
        hidden_raw, last_row = sb("hidden_raw", [P, P]), sb("last_row", [P, 1])
        one = sb("one", [P, 1])
        z = [ps(f"z{b}", [P, 512]) for b in range(ZB)]
        turned = [ps(f"turned{b}", [P, 512]) for b in range(TB)]
        acc = [ps(f"acc{b}", [P, 512]) for b in range(2)]

        const_in, const_ready = sem("a_const_in"), sem("a_const_ready")
        raw_in, v_in = sem("a_raw_in"), sem("a_v_in")
        pool_step, qk_ready, v_ready = sem("a_pool_step"), sem("a_qk_ready"), sem("a_v_ready")
        logits_done, keep_done, scanned = sem("a_logits"), sem("a_keep"), sem("a_scanned")
        turn_done, high_done, low_done, value_done = sem("a_turned"), sem("a_high"), sem("a_low"), sem("a_values")
        half_done, total_done, y_done = sem("a_half"), sem("a_total"), sem("a_y")
        gate_in = [sem(f"a_gate_in{b}") for b in range(2)]
        y_sent = [sem(f"a_y_sent{b}") for b in range(2)]
        block = ctx.enter_context(nc.Block())
        GATES = 2 * GROUPS

        def done(per, i, k):
            return per * (i + 1) + k + 1

        def place(g, qt):
            return sum(keys_of(x) for x in range(GROUP * rank(g), qt))

        def key_tile(kt):
            return (0, META) if kt < 0 else (META + P * kt, P)

        def seen_by(g, kt):
            return max(0, kt - GROUP * rank(g))

        @block.sync
        def _(sp):
            sp.dma_start(hidden_raw[:, :], io["hidden"]).then_inc(const_in, 16)
            sp.dma_start(last_row[:, :], io["last_row"]).then_inc(const_in, 16)
            sp.wait_ge(const_ready, 2)
            with sp.Fori(0, HEADS) as head:
                qrow, krow, cols = bass.ds(DH * head, DH), bass.ds(D + DH * head, DH), bass.ds(DH * head, DH)
                sp.wait_ge(qk_ready, head + 2)
                for half in range(2):
                    rows = slice(DH * half, DH * half + DH)
                    sp.dma_start(q_raw[rows, :], scratch["qk"][qrow, CHUNK:TOK]).then_inc(raw_in, 16)
                    sp.dma_start(k_raw[rows, :], scratch["qk"][krow, PAD:TOK]).then_inc(raw_in, 16)
                sp.wait_ge(v_ready, head + 2)
                for shift, dst in ((0, v_now), (1, v_before)):
                    sp.dma_start(dst[0:META, 0, :], scratch["v_sb"][PAD - shift:CHUNK - shift, cols]).then_inc(v_in, 16)
                    sp.dma_start(dst[:, 1:, :], scratch["v_sb"][CHUNK - shift:TOK - shift, cols].rearrange(
                        "(k p) c -> p k c", p=P)).then_inc(v_in, 16)

        @block.gpsimd
        def _(pool):
            pool.sem_inc(qk_ready, 2)
            pool.sem_inc(v_ready, 2)
            pool.memset(v_now[:, 0, :], 0.0).then_inc(const_ready, 1)
            pool.memset(v_before[:, 0, :], 0.0).then_inc(const_ready, 1)
            pool.wait_ge(const_in, 32)
            pool.tensor_copy(hidden[:, :], hidden_raw[:, :]).then_inc(const_ready, 1)
            pool.memset(one[:, :], 1.0).then_inc(const_ready, 1)
            pool.wait_ge(const_ready, 4)
            pool.tensor_copy(eye[:, :], t["identity"][:, :]).then_inc(const_ready, 1)

            def rounded(out, x):
                ones = one[:, 0:1]
                for size in x.shape[1:-1]:
                    ones = ones.unsqueeze(1)
                return pool.tensor_tensor(out, x, ones.broadcast_to(x.shape), ALU.mult)

            with pool.Fori(0, PAIRS) as i:
                for u in range(2):
                    head = 2 * i + u
                    step = 9 * head
                    low = slice(DH, P)
                    pool.wait_ge(raw_in, 64 * head + 64)
                    pool.wait_ge(value_done, done(n_values, i, last_values[GROUPS * (u + 1) - 1] - n_values))
                    rounded(q_parts[u][:, :], q_raw[:, :]).then_inc(pool_step, 1)
                    pool.wait_ge(pool_step, step + 1)
                    pool.tensor_tensor(q_parts[u][low, :], q_raw[low, :], q_parts[u][low, :].bitcast(F32),
                                       ALU.subtract).then_inc(pool_step, 1)
                    pool.wait_ge(pool_step, step + 2)
                    rounded(k_high[u][:, :], k_raw[:, :]).then_inc(pool_step, 1)
                    pool.wait_ge(pool_step, step + 3)
                    pool.tensor_tensor(k_low[u][:, :], k_raw[:, :], k_high[u][:, :].bitcast(F32),
                                       ALU.subtract).then_inc(qk_ready, 1)
                    pool.wait_ge(qk_ready, head + 3)
                    pool.wait_ge(v_in, 64 * head + 64)
                    pool.tensor_tensor(v_diff[:, :, :], v_before[:, :, :], v_now[:, :, :], ALU.subtract).then_inc(pool_step, 1)
                    pool.wait_ge(pool_step, step + 4)
                    rounded(dv[u][:, :, 0, :], v_diff[:, :, :]).then_inc(pool_step, 1)
                    pool.wait_ge(pool_step, step + 5)
                    pool.tensor_tensor(dv[u][:, :, 1, :], v_diff[:, :, :], dv[u][:, :, 0, :].bitcast(F32),
                                       ALU.subtract).then_inc(pool_step, 1)
                    pool.wait_ge(pool_step, step + 6)
                    pool.tensor_tensor(v_now[:, 1:, :], v_now[:, 1:, :],
                                       last_row[:, :].unsqueeze(1).broadcast_to([P, QT, DH]), ALU.mult).then_inc(pool_step, 1)
                    pool.wait_ge(pool_step, step + 7)
                    pool.tensor_tensor(v_diff[:, 1:, :], v_before[:, 1:, :], v_now[:, 1:, :], ALU.subtract).then_inc(pool_step, 1)
                    pool.wait_ge(pool_step, step + 8)
                    rounded(dv_diag[u][:, :, 0, :], v_diff[:, 1:, :]).then_inc(pool_step, 1)
                    pool.wait_ge(pool_step, step + 9)
                    pool.tensor_tensor(dv_diag[u][:, :, 1, :], v_diff[:, 1:, :], dv_diag[u][:, :, 0, :].bitcast(F32),
                                       ALU.subtract).then_inc(v_ready, 1)
                    pool.wait_ge(v_ready, head + 3)

        @block.tensor
        def _(pe):
            pe.sem_inc(value_done, n_values)
            pe.sem_inc(turn_done, n_values)
            pe.wait_ge(const_ready, 5)
            with pe.Fori(0, PAIRS) as i:
                def logits(g, qt, k0, size, num):
                    u = g // GROUPS
                    pe.wait_ge(qk_ready, done(2, i, u))
                    pe.wait_ge(keep_done, done(n_logits, i, num - ZB))
                    diagonal = k0 + size == keys_of(qt)
                    out = z[num % ZB][:, 0:size]
                    queries = q_parts[u][:, P * qt:P * qt + P]
                    pe.matmul(out, queries, k_high[u][:, k0:k0 + size], start=True, stop=False)
                    mm = pe.matmul(out, queries, k_low[u][:, k0:k0 + size], start=False, stop=not diagonal)
                    if diagonal:
                        mm = pe.matmul(z[num % ZB][:, size - P:size], eye[:, :], hidden[:, :], start=False, stop=True)
                    mm.then_inc(logits_done, 1)

                def turn(g, kt, num):
                    if kt < 0:
                        pe.wait_ge(scanned, done(n_logits, i, last_logits[g]))
                    pe.wait_ge(low_done, done(n_values, i, num - TB))
                    at, size = key_tile(kt)
                    for r in range(seen_by(g, kt), GROUP):
                        qt = GROUP * rank(g) + r
                        src = place(g, qt) + at
                        mm = pe.transpose(turned[num % TB][0:size, P * r:P * r + P], kept[g % 2][:, src:src + size],
                                          t["identity"][:, :])
                    mm.then_inc(turn_done, 1)

                def values(g, kt, num):
                    u, b = g // GROUPS, num % TB
                    pe.wait_ge(low_done, done(n_values, i, num))
                    if kt < 0:
                        pe.wait_ge(v_ready, done(2, i, u))
                        pe.wait_ge(total_done, done(GATES, i, g - 2))
                    _, size = key_tile(kt)
                    r = seen_by(g, kt)
                    out = acc[g % 2]
                    own = kt - GROUP * rank(g) >= 0
                    last = kt == GROUP * (rank(g) + 1) - 1
                    c0 = P * r
                    for part in (w_high, w_low):
                        if own:
                            mm = pe.matmul(out[:, c0:c0 + P], dv_diag[u][:, kt, :, :], part[b][:, c0:c0 + P],
                                           start=False, stop=last and part is w_low)
                        c1 = c0 + P if own else c0
                        if c1 < 512:
                            mm = pe.matmul(out[:, c1:512], dv[u][0:size, kt + 1, :, :], part[b][0:size, c1:512],
                                           start=kt < 0 and part is w_high, stop=False)
                    mm.then_inc(value_done, 1)

                late = []
                for e in order:
                    if e[0] == "logits":
                        logits(*e[1:])
                    else:
                        turn(*e[1:])
                        late.append(e[1:])
                        if len(late) > LAG:
                            values(*late.pop(0))
                for e in late:
                    values(*e)

        @block.scalar
        def _(act):
            act.sem_inc(keep_done, n_logits)
            act.sem_inc(half_done, GATES)
            for b in range(2):
                act.sem_inc(y_sent[b], 16 * GROUPS)
            with act.Fori(0, PAIRS) as i:
                def load_gate(g):
                    rows = bass.ds(D + DH * (2 * i + g // GROUPS), DH)
                    at = 512 * rank(g)
                    act.wait_ge(y_done, done(GATES, i, g - 2))
                    act.dma_start(gate[g % 2][:, :], scratch["gates"][rows, at:at + 512]).then_inc(gate_in[g % 2], 16)

                def store_y(g):
                    rows = bass.ds(D + DH * (2 * i + g // GROUPS), DH)
                    at = 512 * rank(g)
                    act.wait_ge(y_done, done(GATES, i, g))
                    act.dma_start(scratch["y"][rows, at:at + 512], y[g % 2][:, :]).then_inc(y_sent[g % 2], 16)

                load_gate(0)
                load_gate(1)
                for e in finishing(order, last_values, LAG):
                    if e[0] == "logits":
                        _, g, qt, k0, size, num = e
                        act.wait_ge(logits_done, n_logits * i + num + 1)
                        act.wait_ge(scanned, done(n_logits, i, num - KB))
                        act.activation(keep[num % KB][:, 0:size], z[num % ZB][:, 0:size], ACT.Sigmoid,
                                       scale=-DH ** -0.5).then_inc(keep_done, 1)
                    elif e[0] == "values":
                        _, g, kt, num = e
                        _, size = key_tile(kt)
                        c0 = P * seen_by(g, kt)
                        act.wait_ge(turn_done, done(n_values, i, num))
                        act.wait_ge(value_done, done(n_values, i, num - TB))
                        act.copy(w_high[num % TB][0:size, c0:512], turned[num % TB][0:size, c0:512]).then_inc(high_done, 1)
                    else:
                        g = e[1]
                        act.wait_ge(value_done, done(n_values, i, last_values[g]))
                        act.wait_ge(total_done, done(GATES, i, g - 1))
                        act.copy(low_half[:, :], acc[g % 2][DH:P, :]).then_inc(half_done, 1)
                        if g >= 1:
                            store_y(g - 1)
                            if g + 1 < GATES:
                                load_gate(g + 1)
                store_y(GATES - 1)
            for b in range(2):
                act.wait_ge(y_sent[b], 16 * GROUPS * (PAIRS + 1))

        @block.vector
        def _(dve):
            dve.sem_inc(scanned, n_logits)
            dve.sem_inc(low_done, n_values)
            dve.sem_inc(total_done, GATES)
            dve.sem_inc(y_done, GATES)
            with dve.Fori(0, PAIRS) as i:
                for e in finishing(order, last_values, LAG):
                    if e[0] == "logits":
                        _, g, qt, k0, size, num = e
                        at = place(g, qt)
                        end = at + k0 + size
                        first = k0 + size == keys_of(qt)
                        dve.wait_ge(keep_done, done(n_logits, i, num))
                        if first and qt % GROUP == 0:
                            dve.wait_ge(turn_done, done(n_values, i, last_values[g - 2] if g >= 2 else
                                                        last_values[GATES + g - 2] - n_values))
                        if not first:
                            dve.wait_ge(scanned, done(n_logits, i, num - 1))
                        data = keep[num % KB][:, 0:size][:, ::-1]
                        dve.tensor_tensor_scan(kept[g % 2][:, end - size:end][:, ::-1], data, data,
                                               1.0 if first else kept[g % 2][:, end:end + 1],
                                               ALU.mult, ALU.bypass).then_inc(scanned, 1)
                    elif e[0] == "values":
                        _, g, kt, num = e
                        _, size = key_tile(kt)
                        c0 = P * seen_by(g, kt)
                        dve.wait_ge(high_done, n_values * i + num + 1)
                        dve.tensor_tensor(w_low[num % TB][0:size, c0:512], turned[num % TB][0:size, c0:512],
                                          w_high[num % TB][0:size, c0:512].bitcast(F32), ALU.subtract).then_inc(low_done, 1)
                    else:
                        g = e[1]
                        dve.wait_ge(half_done, done(GATES, i, g))
                        dve.tensor_tensor(total[:, :], acc[g % 2][0:DH, :], low_half[:, :], ALU.add).then_inc(total_done, 1)
                        dve.wait_ge(total_done, done(GATES, i, g))
                        dve.wait_ge(gate_in[g % 2], 16 * (GROUPS * i + g // 2 + 1))
                        dve.wait_ge(y_sent[g % 2], 16 * (GROUPS * (i + 1) + g // 2))
                        dve.tensor_tensor(y[g % 2][:, :], total[:, :], gate[g % 2][:, :], ALU.mult).then_inc(y_done, 1)


LEVELS = [2, 4, 8, 16, 32]
HALVES = 2
HP = PAIRS // HALVES
MU, MU_LORA, W0, A0, K_K, K_A, R_K, GN_G, GN_B = 0, 24, 25, 33, 41, 49, 57, 65, 73
N_PARAMS = 81


def rwkv_phase(nc, sem, t, io, scratch):
    with ExitStack() as ctx:
        sb = lambda name, shape, dt=F32: ctx.enter_context(nc.sbuf_tensor(name, shape, dt))
        C = CHUNK
        grid = [P, PAIRS, C]
        par, up = sb("par", [P, N_PARAMS]), sb("up", [P, D])
        omka_eps = sb("omka_eps", [P, 1])
        omka = sb("omka", [P, PAIRS])
        tri, full = sb("tri", [P, 1 + len(LEVELS), P]), sb("full", [P, P])
        ones_sum, ones_mean, restart = sb("ones_sum", [P, P]), sb("ones_mean", [P, P]), sb("restart", [P, PAIRS * C])
        u_in, lora_in = sb("u_in", [P, 3 * PAIRS, C + 1]), sb("lora_in", [P, C + 1])
        gate, y_out = sb("gate", grid), sb("y_out", grid)
        rk_dif, rk = sb("rk_dif", [P, 2 * PAIRS, C]), sb("rk", [P, 2 * PAIRS, C])
        v_dif, v_mix = sb("v_dif", grid), sb("v_mix", grid)
        lora_dif, lora = sb("lora_dif", [P, C]), sb("lora", [DH, C])
        lora_parts = sb("lora_parts", [P, 2, C])
        logits, sig = sb("logits", [P, PAIRS, 2, C]), sb("sig", [P, 2, PAIRS, C])
        run, run_before = sb("run", [P, PAIRS * C]), sb("run_before", [P, PAIRS * C])
        w_now, w_inv, w_before = sb("w_now", grid), sb("w_inv", grid), sb("w_before", grid)
        w_end = [sb(f"w_end{b}", [P, PAIRS]) for b in range(2)]
        kq, kq_sq, k_norm, k_rnorm, kk = sb("kq", grid), sb("kq_sq", grid), sb("k_norm", grid), sb("k_rnorm", grid), sb("kk", grid)
        k_gain, k_fin, r_bonus, kka = sb("k_gain", grid), sb("k_fin", grid), sb("r_bonus", grid), sb("kka", grid)
        bonus, bonus_v = sb("bonus", grid), [sb(f"bonus_v{b}", grid) for b in range(2)]
        AR = [sb(f"AR{b}", [P, PAIRS, 2, 2, C]) for b in range(2)]
        KB = [sb(f"KB{b}", [P, PAIRS, 2, C]) for b in range(2)]
        KBt = sb("KBt", [P, PAIRS, 2, DH])
        VU = sb("VU", [P, PAIRS, 2, DH])
        scores = sb("scores", [P, PAIRS, 2, 2, C])
        NT = sb("NT", grid)
        off = sb("off", [P, len(LEVELS), PAIRS, P])
        T2 = sb("T2", [P, HALVES, 2, HP, P])
        X = sb("X", [P, PAIRS, P])
        LV, R, S, S_sum = sb("LV", grid), sb("R", grid), sb("S", grid), sb("S_sum", grid)
        ysb, yc, yc_sq, y_std, y_rstd = sb("ysb", grid), sb("yc", grid), sb("yc_sq", grid), sb("y_std", grid), sb("y_rstd", grid)
        bank = [ctx.enter_context(nc.psum_tensor(f"rb{b}", [P, 512], F32)) for b in range(8)]

        def row(at, n=PAIRS, width=C):
            return par[:, at:at + n].unsqueeze(2).broadcast_to([P, n, width])

        def as_grid(b, n=PAIRS):
            return bank[b][:, 0:n * C].rearrange("p (k c) -> p k c", k=n)

        names = """pe_go const_in const_ready u_in_ready v_in_ready lora_in_ready gate_in y_sent
            rk_dif rk_scaled rk_mixed lora_dif lora_mixed tanh_done dve_logits logits_pe sig_done run_done run_before_done
            exp_done kq_done kq_sq_done norm_pe norm_done rnorm_done kk_done
            gain gain2 k_fin_done r_bonus1 r_bonus_done kka_done bonus_pe bonus_out bonus_v_done
            v_dif v_scaled v_mixed a_done r_first r_done k_done b_done w_end_done
            kbt_pe kbt_out vt_pe vt_out nt_pe nt_out tt_first tt_init first_pe t_init off_done
            st_pe st_out x_pe x_out t_pe t_out turn_pe tt_out lv_pe lv_out r_pe r_out u_pe u_out0 u_out1 s_pe s_sum s_done
            y_pe ysb_out mean_pe yc_done yc_sq_done var_pe std_done rstd_done y_n1 y_n2 y_n3 y_n4 y_done"""
        s = {name: sem("r_" + name) for name in names.split()}
        block = ctx.enter_context(nc.Block())

        def ready(eng, name, n, k=0, per=1):
            eng.wait_ge(s[name], per * n + k + 1)

        def walk(eng, body, head=None, tail=None):
            assert NCH % 2
            if head:
                head()
            body(0, 0, False, True)
            body(1, 1, False, True)
            with eng.Fori(1, NCH // 2) as i:
                for b in range(2):
                    body(2 * i + b, b, True, True)
            body(NCH - 1, 0, True, False)
            if tail:
                tail()

        def operands_free(eng, n):
            if isinstance(n, int) and n < 2:
                return
            if isinstance(n, int) and n == 2:
                ready(eng, "s_pe", 0, 1, 2)
            else:
                ready(eng, "y_pe", n - 3, 1, 2)

        def out_of(n):
            return not (isinstance(n, int) and n == 0)

        def again(n):
            return not (isinstance(n, int) and n == 0)

        @block.sync
        def _(sp):
            sp.dma_start(par[:, :], io["params"]).then_inc(s["const_in"], 16)
            sp.dma_start(up[:, :], io["up"]).then_inc(s["const_in"], 16)
            sp.dma_start(tri[:, :, :], io["tri"].rearrange("p (k c) -> p k c", c=P)).then_inc(s["const_in"], 16)
            sp.dma_start(full[:, :], io["full"]).then_inc(s["const_in"], 16)
            sp.dma_start(ones_sum[:, :], io["ones_sum"]).then_inc(s["const_in"], 16)
            sp.dma_start(restart[:, :], io["restart"]).then_inc(s["const_in"], 16)

            def load(n):
                if again(n):
                    ready(sp, "rk_mixed", n - 1)
                src = scratch["u"][0:3 * D, bass.ds(C * n, C + 1)].rearrange("(k p) c -> p k c", p=P)
                sp.dma_start(u_in[:, 0:2 * PAIRS, :], src[:, 0:2 * PAIRS, :]).then_inc(s["u_in_ready"], 16)
                if again(n):
                    ready(sp, "v_mixed", n - 1)
                    ready(sp, "lora_mixed", n - 1)
                sp.dma_start(lora_in[:, :], scratch["u"][3 * D:3 * D + P, bass.ds(C * n, C + 1)]).then_inc(s["lora_in_ready"], 16)
                sp.dma_start(u_in[:, 2 * PAIRS:, :], src[:, 2 * PAIRS:, :]).then_inc(s["v_in_ready"], 16)

            def store(n):
                ready(sp, "y_done", n - 1)
                sp.dma_start(scratch["y"][0:D, bass.ds(C * n - C, C)].rearrange("(k p) c -> p k c", p=P),
                             y_out[:, :, :]).then_inc(s["y_sent"], 16)

            def load_gate(n):
                sp.dma_start(gate[:, :, :], scratch["gates"][0:D, bass.ds(C * n - C, C)].rearrange(
                    "(k p) c -> p k c", p=P)).then_inc(s["gate_in"], 16)

            def body(n):
                load(n + 1)
                if not isinstance(n, int) or n > 2:
                    store(n - 2)
                if not isinstance(n, int) or n > 1:
                    load_gate(n - 1)

            load(0)
            for n in range(4):
                body(n)
            with sp.Fori(4, NCH - 1) as n:
                body(n)
            for n in (NCH - 1, NCH):
                store(n - 2)
                load_gate(n - 1)
            store(NCH - 1)
            sp.wait_ge(s["y_sent"], 16 * (NCH - 1))

        @block.tensor
        def _(pe):
            def low_rank(n, means=False):
                ready(pe, "tanh_done", n)
                ready(pe, "lora_mixed", n)
                if again(n):
                    ready(pe, "norm_done", n - 1)
                    if out_of(n - 1):
                        ready(pe, "bonus_out", n - 2)
                    if means:
                        ready(pe, "yc_done", n - 3)
                for k in range(PAIRS):
                    mm = pe.matmul(bank[k // HP][:, P * (k % HP):P * (k % HP) + P], up[:, P * k:P * k + P],
                                   lora_parts[:, :, :].rearrange("p a c -> p (a c)"), start=True, stop=True)
                mm.then_inc(s["logits_pe"], 1)

            def key_norm(n):
                ready(pe, "kq_sq_done", n)
                ready(pe, "dve_logits", n)
                pe.matmul(bank[0][:, :], ones_sum[:, :], kq_sq[:, :, :], start=True, stop=True).then_inc(s["norm_pe"], 1)

            def bonus_sum(n):
                ready(pe, "r_bonus_done", n)
                pe.matmul(bank[1][:, :], ones_sum[:, :], r_bonus[:, :, :], start=True, stop=True).then_inc(s["bonus_pe"], 1)

            def both(f):
                for k in range(PAIRS):
                    for h in range(2):
                        f(k, h, slice(DH * h, DH * h + DH))

            def go():
                pe.sem_inc(s["pe_go"], 1)

            def body(n, b, prev_out, prep):
                for name in ("a_done", "r_done", "k_done", "b_done"):
                    ready(pe, name, n)
                if again(n):
                    ready(pe, "u_out0", n - 1, 1, 2)
                    ready(pe, "u_out1", n - 1, 1, 2)
                go()
                for k in range(PAIRS):
                    for h in range(2):
                        hs = slice(DH * h, DH * h + DH)
                        mm = pe.matmul(bank[6][hs, C * k:C * k + C], KB[b][hs, k, 1, :], AR[b][hs, k, h, 0, :], start=True, stop=True)
                mm.then_inc(s["nt_pe"], 1)
                if again(n):
                    ready(pe, "s_sum", n - 1)
                for k in range(PAIRS):
                    mm = pe.transpose(bank[2 + k // HP][:, P * (k % HP):P * (k % HP) + P],
                                      KB[b][:, k, :, :].rearrange("p a c -> p (a c)"), t["identity"][:, :])
                mm.then_inc(s["kbt_pe"], 1)
                ready(pe, "v_mixed", n)
                if again(n) and out_of(n - 1):
                    ready(pe, "ysb_out", n - 2, 1, 2)
                go()
                for k in range(PAIRS):
                    mm = pe.transpose(bank[4 + k // HP][0:C, P * (k % HP):P * (k % HP) + P], v_mix[:, k, :],
                                      t["identity"][:, :])
                mm.then_inc(s["vt_pe"], 1)
                ready(pe, "kbt_out", n, 1, 2)
                for k in range(PAIRS):
                    if k == HP:
                        ready(pe, "vt_out", n, 1, 2)
                    mm = pe.matmul(bank[2 + k // 2][:, 2 * P * (k % 2):2 * P * (k % 2 + 1)],
                                   KB[b][:, k, :, :].rearrange("p a c -> p (a c)"),
                                   AR[b][:, k, :, :, :].rearrange("p h a c -> p (h a c)"), start=True, stop=True)
                    if k % 2:
                        mm.then_inc(s["st_pe"], 1)

                def beside(lv):
                    if lv == 0 and prep:
                        low_rank(n + 1, prev_out)
                    if lv == 1:
                        if prep:
                            key_norm(n + 1)
                        if prev_out:
                            ready(pe, "yc_sq_done", n - 2)
                            pe.matmul(bank[1][:, :], ones_mean[:, :], yc_sq[:, :, :], start=True, stop=True).then_inc(s["var_pe"], 1)

                    if lv == len(LEVELS) - 1:
                        ready(pe, "vt_out", n, 1, 2)
                        go()
                        for k in range(PAIRS):
                            for h in range(2):
                                mm = pe.matmul(bank[6][DH * h:DH * h + DH, C * k:C * k + C], scores[0:DH, k, h, 0, :],
                                               VU[0:DH, k, h, :], start=True, stop=True)
                        mm.then_inc(s["lv_pe"], 1)

                for half in range(HALVES):
                    ready(pe, "tt_init", n, half, 2)
                    for k in range(HP):
                        mm = pe.transpose(bank[7 - half][:, P * k:P * k + P], T2[:, half, 1, k, :], t["identity"][:, :])
                    mm.then_inc(s["first_pe"], 1)
                if out_of(n):
                    bonus_sum(n)
                if prev_out:
                    ready(pe, "norm_done", n)
                    pe.matmul(bank[0][:, :], ones_mean[:, :], ysb[:, :, :], start=True, stop=True).then_inc(s["mean_pe"], 1)
                ready(pe, "st_out", n, 3, 4)
                for lv in range(len(LEVELS)):
                    last = lv == len(LEVELS) - 1
                    ready(pe, "off_done", n, lv, len(LEVELS))
                    for half in range(HALVES):
                        if lv:
                            ready(pe, "t_out", n, 2 * (lv - 1) + half, 10)
                        else:
                            ready(pe, "t_init", n, half, 2)
                        for k in range(HP):
                            mm = pe.matmul(bank[2 + half][:, P * k:P * k + P], off[:, lv, HP * half + k, :],
                                           T2[:, half, 0, k, :], start=True, stop=True)
                        mm.then_inc(s["x_pe"], 1)
                    if lv:
                        if lv == 1:
                            ready(pe, "t_init", n, 1, 2)
                        for half in range(HALVES):
                            for k in range(HP):
                                mm = pe.transpose(bank[6 + half][:, P * k:P * k + P], T2[:, half, 0, k, :],
                                                  t["identity"][:, :])
                            mm.then_inc(s["turn_pe"], 1)
                    for half in range(HALVES):
                        ready(pe, "x_out", n, 2 * lv + half, 10)
                        if lv:
                            ready(pe, "tt_out", n, 2 * (lv - 1) + half, 8)
                        for k in range(HP):
                            dst, x, tt_ = bank[4 + half][:, P * k:P * k + P], X[:, HP * half + k, :], T2[:, half, 1, k, :]
                            mm = pe.matmul(dst, x, tt_, start=True, stop=True) if last else pe.matmul(
                                dst, tt_, x, start=True, stop=True)
                        mm.then_inc(s["t_pe"], 1)
                        if half == 0:
                            beside(lv)

                for half in range(HALVES):
                    for k in range(HP):
                        for h in range(2):
                            hs = slice(DH * h, DH * h + DH)
                            mm = pe.matmul(bank[2 + half][hs, C * k:C * k + C], AR[b][hs, HP * half + k, h, 0, :],
                                           S[hs, HP * half + k, :], start=True, stop=True)
                    mm.then_inc(s["r_pe"], 1)
                ready(pe, "lv_out", n)
                for half in range(HALVES):
                    ready(pe, "r_out", n, half, 2)
                    ready(pe, "t_out", n, 9, 10)
                    go()
                    for h in range(2):
                        hs = slice(DH * h, DH * h + DH)
                        for k in range(HP):
                            mm = pe.matmul(bank[4 + 2 * half + h][DH:P, C * k:C * k + C], T2[hs, half, 1, k, hs],
                                           R[hs, HP * half + k, :], start=True, stop=True)
                    mm.then_inc(s["u_pe"], 1)
                for half in range(HALVES):
                    ready(pe, "u_out0", n, half, 2)
                    ready(pe, "u_out1", n, half, 2)
                    for k in range(HP):
                        for h in range(2):
                            mm = pe.matmul(bank[2 + half][DH * h:DH * h + DH, C * k:C * k + C], KBt[:, HP * half + k, h, :],
                                           VU[:, HP * half + k, h, :], start=True, stop=True)
                    mm.then_inc(s["s_pe"], 1)
                if out_of(n):
                    for half in range(HALVES):
                        for k in range(HP):
                            for h in range(2):
                                hs = slice(DH * h, DH * h + DH)
                                kk_ = HP * half + k
                                out = bank[4 + half][hs, C * k:C * k + C]
                                pe.matmul(out, S[hs, kk_, :], AR[b][hs, kk_, h, 1, :], start=True, stop=False)
                                mm = pe.matmul(out, VU[:, kk_, h, :], scores[:, kk_, h, 1, :], start=False, stop=True)
                        mm.then_inc(s["y_pe"], 1)

            def head():
                pe.wait_ge(s["const_ready"], 2)
                low_rank(0)
                key_norm(0)

            def tail():
                n = NCH - 1
                ready(pe, "ysb_out", n - 1, 1, 2)
                ready(pe, "std_done", n - 2)
                pe.matmul(bank[0][:, :], ones_mean[:, :], ysb[:, :, :], start=True, stop=True).then_inc(s["mean_pe"], 1)
                ready(pe, "yc_sq_done", n - 1)
                pe.matmul(bank[1][:, :], ones_mean[:, :], yc_sq[:, :, :], start=True, stop=True).then_inc(s["var_pe"], 1)

            walk(pe, body, head, tail)

        @block.scalar
        def _(act):
            def tanh(n):
                ready(act, "lora_mixed", n)
                if again(n):
                    ready(act, "logits_pe", n - 1)
                act.activation(lora_parts[0:DH, 0, :], lora[:, :], ACT.Tanh).then_inc(s["tanh_done"], 1)

            def square_keys(n):
                ready(act, "kq_done", n)
                if again(n):
                    ready(act, "norm_pe", n - 1)
                act.activation(kq_sq[:, :, :], kq[:, :, :], ACT.Square).then_inc(s["kq_sq_done"], 1)

            def root_keys(n):
                ready(act, "norm_pe", n)
                if again(n):
                    ready(act, "rnorm_done", n - 1, 3, 4)
                act.activation(k_norm[:, :, :], bank[0][:, :], ACT.Sqrt, bias=omka_eps[:, 0:1]).then_inc(s["norm_done"], 1)

            def sigmoids(n):
                ready(act, "dve_logits", n)
                if again(n):
                    ready(act, "kka_done", n - 1)
                    ready(act, "run_before_done", n - 1)
                    ready(act, "gain", n - 1)
                act.activation(sig[:, :, :, :], logits[:, :, :, :].rearrange("p k a c -> p a k c"), ACT.Sigmoid).then_inc(s["sig_done"], 1)

            def decays(n):
                ready(act, "run_before_done", n)
                if again(n):
                    for name in ("a_done", "r_done", "k_done", "b_done", "w_end_done"):
                        ready(act, name, n - 1)
                act.activation(w_now[:, :, :], run[:, :], ACT.Exp, scale=-DECAY_SCALE)
                act.activation(w_inv[:, :, :], run[:, :], ACT.Exp, scale=DECAY_SCALE)
                act.activation(w_before[:, :, :], run_before[:, :], ACT.Exp, scale=-DECAY_SCALE).then_inc(s["exp_done"], 1)

            def square_out(m):
                ready(act, "yc_done", m - 1)
                act.activation(yc_sq[:, :, :], yc[:, :, :], ACT.Square).then_inc(s["yc_sq_done"], 1)

            def root_out(m):
                ready(act, "var_pe", m - 1)
                act.activation(y_std[:, :, :], bank[1][:, :], ACT.Sqrt, bias=t["eps"][:, 1:2]).then_inc(s["std_done"], 1)

            def body(n, b, prev_out, prep):
                ready(act, "nt_pe", n)
                if again(n):
                    ready(act, "off_done", n - 1, 4, 5)
                    ready(act, "tt_first", n - 1, 1, 2)
                act.copy(NT[:, :, :], as_grid(6)).then_inc(s["nt_out"], 1)
                if prep:
                    tanh(n + 1)
                ready(act, "kbt_pe", n)
                for half in range(HALVES):
                    act.copy(KBt[:, HP * half:HP * half + HP, :, :].rearrange("p k h c -> p k (h c)"),
                             bank[2 + half][:, :].rearrange("p (k c) -> p k c", k=HP)).then_inc(s["kbt_out"], 1)
                ready(act, "vt_pe", n)
                for half in range(HALVES):
                    act.copy(VU[0:C, HP * half:HP * half + HP, :, :].rearrange("p k h c -> p k (h c)"),
                             bank[4 + half][0:C, :].rearrange("p (k c) -> p k c", k=HP)).then_inc(s["vt_out"], 1)
                for half in range(HALVES):
                    ready(act, "first_pe", n, half, 2)
                    act.copy(T2[:, half, 0, :, :].rearrange("p k c -> p (k c)"), bank[7 - half][:, :]).then_inc(s["t_init"], 1)
                if out_of(n):
                    ready(act, "bonus_pe", n - 1)
                    if prev_out:
                        ready(act, "bonus_v_done", n - 2)
                    act.copy(bonus[:, :, :], as_grid(1)).then_inc(s["bonus_out"], 1)
                for lv in range(len(LEVELS)):
                    for half in range(HALVES):
                        ready(act, "x_pe", n, 2 * lv + half, 10)
                        act.copy(X[:, HP * half:HP * half + HP, :].rearrange("p k c -> p (k c)"),
                                 bank[2 + half][:, :]).then_inc(s["x_out"], 1)
                    if lv:
                        for half in range(HALVES):
                            ready(act, "turn_pe", n, 2 * (lv - 1) + half, 8)
                            act.copy(T2[:, half, 1, :, :].rearrange("p k c -> p (k c)"), bank[6 + half][:, :]).then_inc(s["tt_out"], 1)
                    if lv == 0:
                        if prep:
                            square_keys(n + 1)
                        if prev_out:
                            square_out(n - 1)
                    if lv == 1 and prep:
                        sigmoids(n + 1)
                    if lv == 2:
                        if prep:
                            root_keys(n + 1)
                        if prev_out:
                            root_out(n - 1)
                    if lv == 3 and prep:
                        decays(n + 1)
                ready(act, "lv_pe", n)
                act.copy(LV[:, :, :], as_grid(6)).then_inc(s["lv_out"], 1)
                for half in range(HALVES):
                    ready(act, "u_pe", n, half, 2)
                    act.copy(VU[DH:P, HP * half:HP * half + HP, 0, :],
                             bank[4 + 2 * half][DH:P, 0:HP * C].rearrange("p (k c) -> p k c", k=HP)).then_inc(s["u_out0"], 1)
                if out_of(n):
                    if prev_out:
                        ready(act, "yc_done", n - 2)
                    for half in range(HALVES):
                        ready(act, "y_pe", n - 1, half, 2)
                        act.copy(ysb[:, HP * half:HP * half + HP, :], as_grid(4 + half, HP)).then_inc(s["ysb_out"], 1)

            def head():
                act.wait_ge(s["const_ready"], 2)
                tanh(0)
                square_keys(0)
                root_keys(0)
                sigmoids(0)
                decays(0)

            def tail():
                square_out(NCH - 1)
                root_out(NCH - 1)

            walk(act, body, head, tail)

        @block.vector
        def _(dve):
            def tt(out, a, b, op, name):
                dve.tensor_tensor(out, a, b, op).then_inc(s[name], 1)

            def mix(n):
                dve.wait_ge(s["u_in_ready"], 16 * n + 16)
                if again(n):
                    for name in ("r_done", "kk_done", "k_fin_done", "r_bonus1"):
                        ready(dve, name, n - 1)
                tt(rk_dif[:, :, :], u_in[:, 0:2 * PAIRS, 0:C], u_in[:, 0:2 * PAIRS, 1:], ALU.subtract, "rk_dif")

            def mix_scale(n):
                ready(dve, "rk_dif", n)
                tt(rk_dif[:, :, :], rk_dif[:, :, :], row(MU, 2 * PAIRS), ALU.mult, "rk_scaled")

            def mix_add(n):
                ready(dve, "rk_scaled", n)
                tt(rk[:, :, :], rk_dif[:, :, :], u_in[:, 0:2 * PAIRS, 1:], ALU.add, "rk_mixed")

            def mix_lora(n):
                dve.wait_ge(s["lora_in_ready"], 16 * n + 16)
                if again(n):
                    ready(dve, "logits_pe", n - 1)
                tt(lora_dif[:, :], lora_in[:, 0:C], lora_in[:, 1:], ALU.subtract, "lora_dif")
                ready(dve, "lora_dif", n)
                for rows, dst in ((slice(0, DH), lora[:, :]), (slice(DH, P), lora_parts[DH:P, 1, :])):
                    i_ = dve.scalar_tensor_tensor(dst, lora_dif[rows, :], par[rows, MU_LORA:MU_LORA + 1],
                                                  lora_in[rows, 1:], ALU.mult, ALU.add)
                i_.then_inc(s["lora_mixed"], 1)

            def keys(n):
                ready(dve, "rk_mixed", n)
                if again(n):
                    ready(dve, "kk_done", n - 1)
                    ready(dve, "kq_sq_done", n - 1)
                tt(kq[:, :, :], rk[:, PAIRS:, :], row(K_K), ALU.mult, "kq_done")

            def add_bias(n):
                ready(dve, "logits_pe", n)
                if again(n):
                    ready(dve, "sig_done", n - 1)
                assert A0 == W0 + PAIRS
                biases = par[:, W0:W0 + 2 * PAIRS].rearrange("p (a k) -> p k a", a=2)
                for half in range(HALVES):
                    ks = slice(HP * half, HP * half + HP)
                    i_ = dve.tensor_tensor(logits[:, ks, :, :], bank[half][:, :].rearrange("p (k a c) -> p k a c", a=2, c=C),
                                           biases[:, ks, :].unsqueeze(3).broadcast_to([P, HP, 2, C]), ALU.add)
                i_.then_inc(s["dve_logits"], 1)

            def running(n):
                ready(dve, "sig_done", n)
                if again(n):
                    ready(dve, "exp_done", n - 1)
                w = sig[:, 0, :, :].rearrange("p k c -> p (k c)")
                dve.tensor_tensor_scan(run[:, :], restart[:, :], w, 0.0, ALU.mult, ALU.add).then_inc(s["run_done"], 1)
                ready(dve, "run_done", n)
                tt(run_before[:, :], run[:, :], w, ALU.subtract, "run_before_done")

            def invert_norms(n, q):
                ready(dve, "norm_done", n)
                ks = slice(2 * q, 2 * q + 2)
                dve.reciprocal(k_rnorm[:, ks, :], k_norm[:, ks, :]).then_inc(s["rnorm_done"], 1)

            def unit_keys(n):
                ready(dve, "rnorm_done", n, 3, 4)
                if again(n):
                    ready(dve, "a_done", n - 1)
                    ready(dve, "kka_done", n - 1)
                tt(kk[:, :, :], kq[:, :, :], k_rnorm[:, :, :], ALU.mult, "kk_done")

            def operand_a(n, b):
                ready(dve, "exp_done", n)
                ready(dve, "kk_done", n)
                operands_free(dve, n)
                dve.tensor_tensor(AR[b][0:DH, :, 0, 0, :], kk[0:DH, :, :], w_before[0:DH, :, :], ALU.mult)
                tt(AR[b][DH:P, :, 1, 0, :], kk[DH:P, :, :], w_before[DH:P, :, :], ALU.mult, "a_done")
                dve.tensor_copy(w_end[b][:, :], w_now[:, :, C - 1]).then_inc(s["w_end_done"], 1)

            def operand_b(n, b):
                ready(dve, "kka_done", n)
                dve.scalar_tensor_tensor(KB[b][:, :, 1, :], kka[:, :, :], -1.0, w_inv[:, :, :], ALU.mult,
                                         ALU.mult).then_inc(s["b_done"], 1)

            def centre(m):
                ready(dve, "mean_pe", m - 1)
                if not isinstance(m, int) or m > 1:
                    ready(dve, "y_n1", m - 2)
                tt(yc[:, :, :], ysb[:, :, :], as_grid(0), ALU.subtract, "yc_done")

            def rstd(m):
                ready(dve, "std_done", m - 1)
                dve.reciprocal(y_rstd[:, :, :], y_std[:, :, :]).then_inc(s["rstd_done"], 1)

            def body(n, b, prev_out, prep):
                def beside(lv):
                    if prep:
                        m = n + 1
                        for at, work in ((0, lambda: add_bias(m)), (1, lambda: running(m)),
                                         (2, lambda: invert_norms(m, 0)), (2, lambda: invert_norms(m, 1)),
                                         (3, lambda: invert_norms(m, 2)), (3, lambda: invert_norms(m, 3)),
                                         (3, lambda: unit_keys(m)), (4, lambda: operand_a(m, 1 - b))):
                            if at == lv:
                                work()

                if prep:
                    mix_lora(n + 1)
                    mix(n + 1)
                    mix_scale(n + 1)
                    mix_add(n + 1)
                    keys(n + 1)
                ready(dve, "nt_out", n)
                blocks = [P, HP, 2, C]
                for half in range(HALVES):
                    ks = slice(HP * half, HP * half + HP)
                    dve.tensor_tensor(T2[:, half, 1, :, :].rearrange("p k (h c) -> p k h c", c=C),
                                      NT[:, ks, :].unsqueeze(2).broadcast_to(blocks),
                                      tri[:, 0, :].rearrange("p (h c) -> p h c", c=C).unsqueeze(1).broadcast_to(blocks),
                                      ALU.mult).then_inc(s["tt_first"], 1)
                for half in range(HALVES):
                    ready(dve, "tt_first", n, half, 2)
                    tt(T2[:, half, 1, :, :], T2[:, half, 1, :, :], t["identity"][:, :].unsqueeze(1).broadcast_to([P, HP, P]),
                       ALU.add, "tt_init")
                for q in range(4):
                    ready(dve, "st_pe", n, q, 4)
                    dve.tensor_tensor(scores[:, 2 * q:2 * q + 2, :, :, :].rearrange("p k h a c -> p (k h) (a c)"),
                                      bank[2 + q][:, :].rearrange("p (k c) -> p k c", c=P),
                                      full[:, :].unsqueeze(1).broadcast_to([P, 4, P]), ALU.mult).then_inc(s["st_out"], 1)
                if prev_out:
                    centre(n - 1)
                for lv in range(len(LEVELS)):
                    last = lv == len(LEVELS) - 1
                    for half in range(HALVES):
                        ready(dve, "t_pe", n, 2 * lv + half, 10)
                        dst = T2[:, half, 1 if last else 0, :, :].rearrange("p k c -> p (k c)")
                        tt(dst, dst, bank[4 + half][:, :], ALU.add, "t_out")
                    beside(lv)
                for half in range(HALVES):
                    ks = slice(HP * half, HP * half + HP)
                    ready(dve, "r_pe", n, half, 2)
                    ready(dve, "lv_out", n)
                    tt(R[:, ks, :], as_grid(2 + half, HP), LV[:, ks, :], ALU.add, "r_out")
                for half in range(HALVES):
                    ready(dve, "u_pe", n, half, 2)
                    dve.tensor_copy(VU[DH:P, HP * half:HP * half + HP, 1, :],
                                    bank[5 + 2 * half][DH:P, 0:HP * C].rearrange("p (k c) -> p k c", k=HP)).then_inc(s["u_out1"], 1)
                if prep:
                    operand_b(n + 1, 1 - b)
                if prev_out:
                    rstd(n - 1)
                ready(dve, "s_pe", n, 1, 2)
                for half in range(HALVES):
                    ks = slice(HP * half, HP * half + HP)
                    i_ = dve.tensor_tensor(S_sum[:, ks, :], as_grid(2 + half, HP), S[:, ks, :], ALU.add)
                i_.then_inc(s["s_sum"], 1)
                ready(dve, "s_sum", n)
                if out_of(n):
                    ready(dve, "y_pe", n - 1, 1, 2)
                tt(S[:, :, :], S_sum[:, :, :], w_end[b][:, :].unsqueeze(2).broadcast_to(grid), ALU.mult, "s_done")

            def head():
                dve.memset(S[:, :, :], 0.0)
                for b in range(2):
                    dve.memset(AR[b][:, :, :, :, :], 0.0)
                dve.memset(lora_parts[:, :, :], 0.0)
                dve.memset(omka_eps[:, 0:1], L2_EPS)
                dve.wait_ge(s["const_in"], 96)
                dve.tensor_scalar(ones_mean[:, :], ones_sum[:, :], 1.0 / DH, None, ALU.mult).then_inc(s["const_ready"], 1)
                dve.tensor_scalar(omka[:, :], par[:, K_A:K_A + PAIRS], -1.0, 1.0, ALU.mult, ALU.add).then_inc(s["const_ready"], 1)
                dve.wait_ge(s["const_ready"], 2)
                mix_lora(0)
                mix(0)
                mix_scale(0)
                mix_add(0)
                keys(0)
                add_bias(0)
                for q in range(4):
                    invert_norms(0, q)
                unit_keys(0)
                running(0)
                operand_a(0, 0)
                operand_b(0, 0)

            def tail():
                centre(NCH - 1)
                rstd(NCH - 1)

            walk(dve, body, head, tail)

        @block.gpsimd
        def _(pool):
            def tt(out, a, b, op, name):
                pool.tensor_tensor(out, a, b, op).then_inc(s[name], 1)

            def mix_v(n):
                pool.wait_ge(s["v_in_ready"], 16 * n + 16)
                if again(n):
                    ready(pool, "vt_pe", n - 1)
                cur, before = u_in[:, 2 * PAIRS:, 1:], u_in[:, 2 * PAIRS:, 0:C]
                tt(v_dif[:, :, :], before, cur, ALU.subtract, "v_dif")
                ready(pool, "v_dif", n)
                tt(v_dif[:, :, :], v_dif[:, :, :], row(MU + 2 * PAIRS), ALU.mult, "v_scaled")
                ready(pool, "v_scaled", n)
                tt(v_mix[:, :, :], v_dif[:, :, :], cur, ALU.add, "v_mixed")

            def final_keys(n):
                ready(pool, "sig_done", n)
                if again(n):
                    ready(pool, "k_done", n - 1)
                    ready(pool, "b_done", n - 1)
                    ready(pool, "bonus_pe", n - 2) if out_of(n - 1) else None
                a = sig[:, 1, :, :]
                tt(k_gain[:, :, :], a, row(K_A), ALU.mult, "gain")
                ready(pool, "gain", n)
                tt(k_gain[:, :, :], k_gain[:, :, :], omka[:, :].unsqueeze(2).broadcast_to(grid), ALU.add, "gain2")
                ready(pool, "gain2", n)
                tt(k_fin[:, :, :], k_gain[:, :, :], rk[:, PAIRS:, :], ALU.mult, "k_fin_done")
                ready(pool, "k_fin_done", n)
                tt(r_bonus[:, :, :], rk[:, 0:PAIRS, :], row(R_K), ALU.mult, "r_bonus1")
                ready(pool, "r_bonus1", n)
                tt(r_bonus[:, :, :], r_bonus[:, :, :], k_fin[:, :, :], ALU.mult, "r_bonus_done")
                ready(pool, "kk_done", n)
                ready(pool, "r_bonus_done", n)
                tt(kka[:, :, :], a, kk[:, :, :], ALU.mult, "kka_done")

            def operands(n, b):
                ready(pool, "exp_done", n)
                ready(pool, "kka_done", n)
                operands_free(pool, n)
                tt(KB[b][:, :, 0, :], k_fin[:, :, :], w_inv[:, :, :], ALU.mult, "k_done")
                ready(pool, "k_done", n)
                tt(AR[b][0:DH, :, 0, 1, :], rk[0:DH, 0:PAIRS, :], w_now[0:DH, :, :], ALU.mult, "r_first")
                ready(pool, "r_first", n)
                tt(AR[b][DH:P, :, 1, 1, :], rk[DH:P, 0:PAIRS, :], w_now[DH:P, :, :], ALU.mult, "r_done")

            def normalise(m, b):
                ready(pool, "rstd_done", m - 1)
                if not isinstance(m, int) or m > 1:
                    pool.wait_ge(s["y_sent"], 16 * (m - 1))
                tt(y_out[:, :, :], yc[:, :, :], y_rstd[:, :, :], ALU.mult, "y_n1")
                ready(pool, "y_n1", m - 1)
                tt(y_out[:, :, :], y_out[:, :, :], row(GN_G), ALU.mult, "y_n2")
                ready(pool, "y_n2", m - 1)
                tt(y_out[:, :, :], y_out[:, :, :], row(GN_B), ALU.add, "y_n3")
                ready(pool, "y_n3", m - 1)
                tt(y_out[:, :, :], y_out[:, :, :], bonus_v[b][:, :, :], ALU.add, "y_n4")
                ready(pool, "y_n4", m - 1)
                pool.wait_ge(s["gate_in"], 16 * m)
                tt(y_out[:, :, :], y_out[:, :, :], gate[:, :, :], ALU.mult, "y_done")

            def body(n, b, prev_out, prep):
                ready(pool, "nt_out", n)
                if again(n):
                    ready(pool, "u_pe", n - 1, 1, 2)
                    ready(pool, "r_done", n)
                blocks = [P, PAIRS, 2, C]
                for lv in range(len(LEVELS)):
                    tt(off[:, lv, :, :].rearrange("p k (h c) -> p k h c", c=C), NT[:, :, :].unsqueeze(2).broadcast_to(blocks),
                       tri[:, 1 + lv, :].rearrange("p (h c) -> p h c", c=C).unsqueeze(1).broadcast_to(blocks), ALU.mult, "off_done")
                    ready(pool, "off_done", n, lv, len(LEVELS))
                if out_of(n):
                    ready(pool, "bonus_out", n - 1)
                    tt(bonus_v[b][:, :, :], bonus[:, :, :], v_mix[:, :, :], ALU.mult, "bonus_v_done")
                    ready(pool, "bonus_v_done", n - 1)
                if prep:
                    mix_v(n + 1)
                    ready(pool, "v_mixed", n + 1)
                    final_keys(n + 1)
                    operands(n + 1, 1 - b)
                    ready(pool, "r_done", n + 1)
                if prev_out:
                    normalise(n - 1, 1 - b)
                    ready(pool, "y_done", n - 2)

            def head():
                pool.wait_ge(s["const_ready"], 2)
                final_keys(0)
                mix_v(0)
                ready(pool, "v_mixed", 0)
                operands(0, 0)

            def tail():
                normalise(NCH - 1, 0)

            walk(pool, body, head, tail)



GT = 512
Y_SLOTS, M_SLOTS = 4, 4
OT = 256


def branch_phase(nc, sem, t, io, scratch, w_out_first):
    with ExitStack() as ctx:
        sb = lambda name, shape, dt=F32: ctx.enter_context(nc.sbuf_tensor(name, shape, dt))
        w_hi, w_lo = sb("proj_hi", [P, 2 * KC, D], F32R), sb("proj_lo", [P, 2 * KC, D], F32R)
        w_raw = [sb(f"proj_raw{b}", [P, D]) for b in range(2)]
        y_raw = [sb(f"y_raw{b}", [P, GT]) for b in range(Y_SLOTS)]
        y_hi = [sb(f"y_hi{b}", [P, GT], F32R) for b in range(Y_SLOTS)]
        y_lo = [sb(f"y_lo{b}", [P, GT], F32R) for b in range(Y_SLOTS)]
        gate = [sb(f"merge{b}", [P, GT]) for b in range(M_SLOTS)]
        mixed = sb("mixed", [P, KC, GT])
        bank = [ctx.enter_context(nc.psum_tensor(f"bb{b}", [P, GT], F32)) for b in range(KC)]
        w_in = [sem(f"b_w_in{b}") for b in range(2)]
        y_in = [sem(f"b_y_in{b}") for b in range(Y_SLOTS)]
        gate_in = [sem(f"b_gate_in{b}") for b in range(M_SLOTS)]
        w_high, w_low, y_high, y_low = sem("b_w_high"), sem("b_w_low"), sem("b_y_high"), sem("b_y_low")
        chunk_used, product = sem("b_chunk_used"), sem("b_product")
        gated, mixed_done, mixed_sent = sem("b_gated"), sem("b_mixed"), sem("b_mixed_sent")
        w_out_in = sem("b_w_out_in")
        block = ctx.enter_context(nc.Block())
        CH = 2 * KC

        def walk(eng, body):
            body(0, True)
            with eng.Fori(1, SEQ // GT) as g:
                body(g, False)

        def used(eng, g, c):
            r, k = divmod(c, KC)
            if k == KC - 1:
                eng.wait_ge(product, CH * g + KC * (r + 1))
            else:
                eng.wait_ge(chunk_used, (KC - 1) * (2 * g + r) + k + 1)

        @block.sync
        def _(sp):
            def load_gate(g, e):
                if e >= 0 and (not isinstance(g, int) or e >= M_SLOTS):
                    if M_SLOTS <= e < M_SLOTS + KC:
                        sp.wait_ge(gated, CH * g + e - M_SLOTS + 1)
                    elif e < M_SLOTS:
                        sp.wait_ge(mixed_done, KC * g + e - M_SLOTS + 1)
                    else:
                        sp.wait_ge(mixed_done, KC * g + e - KC - M_SLOTS + 1)
                sp.dma_start(gate[e % M_SLOTS][:, :], scratch["merge"][P * e:P * e + P, bass.ds(GT * g, GT)]).then_inc(
                    gate_in[e % M_SLOTS], 16)

            def load_weights(c):
                if c >= 2:
                    sp.wait_ge(w_low, c - 1)
                sp.dma_start(w_raw[c % 2][:, :], io["w_proj"][P * c:P * c + P, :]).then_inc(w_in[c % 2], 16)

            load_weights(0)
            load_weights(1)

            def body(g, first):
                for c in range(CH):
                    if not first or c >= Y_SLOTS:
                        sp.wait_ge(y_low, CH * g + c - Y_SLOTS + 1)
                    if first and c >= 2:
                        load_weights(c)
                    sp.dma_start(y_raw[c % Y_SLOTS][:, :],
                                 scratch["y"][P * c:P * c + P, bass.ds(GT * g, GT)]).then_inc(y_in[c % Y_SLOTS], 16)
                    if c == 2 and not first:
                        for m in range(4, KC):
                            load_gate(g - 1, KC + m)
                    if c == KC + 2:
                        for m in range(4, KC):
                            load_gate(g, m)
                    if 3 <= c < 7:
                        load_gate(g, c - 3)
                    if KC + 3 <= c < KC + 7:
                        load_gate(g, c - 3)

            walk(sp, body)
            for m in range(4, KC):
                load_gate(SEQ // GT - 1, KC + m)

        @block.scalar
        def _(act):
            def store(g):
                for m in range(KC):
                    act.wait_ge(mixed_done, KC * g + m + 1)
                    act.dma_start(scratch["mixed"][P * m:P * m + P, bass.ds(GT * g, GT)], mixed[:, m, :]).then_inc(mixed_sent, 16)

            def body(g, first):
                for c in range(CH):
                    if first:
                        act.wait_ge(w_in[c % 2], 16 * (c // 2) + 16)
                        act.copy(w_hi[:, c, :], w_raw[c % 2][:, :]).then_inc(w_high, 1)
                    if not first or c >= Y_SLOTS:
                        used(act, g, c - Y_SLOTS)
                    act.wait_ge(y_in[c % Y_SLOTS], 16 * (CH // Y_SLOTS * g + c // Y_SLOTS) + 16)
                    act.copy(y_hi[c % Y_SLOTS][:, :], y_raw[c % Y_SLOTS][:, :]).then_inc(y_high, 1)
                    if c == 4 and not first:
                        store(g - 1)
                if first:
                    act.dma_start(w_out_first[:, :, :], io["w_out"][0:D // 2, :].rearrange("(k p) c -> p k c", p=P)).then_inc(w_out_in, 16)

            walk(act, body)
            store(SEQ // GT - 1)
            act.wait_ge(w_out_in, 16)
            act.wait_ge(mixed_sent, 16 * KC * (SEQ // GT))

        @block.tensor
        def _(pe):
            def body(g, first):
                for c in range(CH):
                    if first:
                        pe.wait_ge(w_low, c + 1)
                    pe.wait_ge(y_low, CH * g + c + 1)
                    k = c % KC
                    for m in range(KC):
                        if k == 0 and not (first and c == 0):
                            pe.wait_ge(gated, CH * g + c - KC + m + 1)
                        cols = slice(P * m, P * m + P)
                        pe.matmul(bank[m][:, :], w_hi[:, c, cols], y_hi[c % Y_SLOTS][:, :], start=k == 0, stop=False)
                        pe.matmul(bank[m][:, :], w_hi[:, c, cols], y_lo[c % Y_SLOTS][:, :], start=False, stop=False)
                        mm = pe.matmul(bank[m][:, :], w_lo[:, c, cols], y_hi[c % Y_SLOTS][:, :], start=False,
                                       stop=k == KC - 1)
                        if k == KC - 1:
                            mm.then_inc(product, 1)
                        elif m == KC - 1:
                            mm.then_inc(chunk_used, 1)

            walk(pe, body)

        @block.vector
        def _(dve):
            def mix(g, r):
                if r == 0 and not isinstance(g, int):
                    dve.wait_ge(mixed_sent, 16 * KC * g)
                for m in range(KC):
                    e = KC * r + m
                    dve.wait_ge(product, CH * g + e + 1)
                    dve.wait_ge(gate_in[e % M_SLOTS], 16 * (CH // M_SLOTS * g + e // M_SLOTS) + 16)
                    dst = gate[e % M_SLOTS][:, :] if r else mixed[:, m, :]
                    dve.tensor_tensor(dst, bank[m][:, :], gate[e % M_SLOTS][:, :], ALU.mult).then_inc(gated, 1)

            def body(g, first):
                for c in range(CH):
                    if first:
                        dve.wait_ge(w_high, c + 1)
                        dve.tensor_tensor(w_lo[:, c, :], w_raw[c % 2][:, :], w_hi[:, c, :].bitcast(F32),
                                          ALU.subtract).then_inc(w_low, 1)
                    dve.wait_ge(y_high, CH * g + c + 1)
                    dve.tensor_tensor(y_lo[c % Y_SLOTS][:, :], y_raw[c % Y_SLOTS][:, :], y_hi[c % Y_SLOTS][:, :].bitcast(F32), ALU.subtract).then_inc(y_low, 1)
                    if c == 1 and not first:
                        mix(g - 1, 1)
                    if c == KC + 1:
                        mix(g, 0)

            walk(dve, body)
            mix(SEQ // GT - 1, 1)

        @block.gpsimd
        def _(pool):
            with pool.Fori(0, SEQ // GT) as g:
                for m in range(KC):
                    pool.wait_ge(gated, CH * g + KC + m + 1)
                    pool.tensor_tensor(mixed[:, m, :], mixed[:, m, :], gate[m % M_SLOTS][:, :], ALU.add).then_inc(mixed_done, 1)


def output_phase(nc, sem, t, io, out, scratch, w_first):
    with ExitStack() as ctx:
        sb = lambda name, shape, dt=F32: ctx.enter_context(nc.sbuf_tensor(name, shape, dt))
        w_second = sb("w_out_second", [P, KC // 2, D])
        w_hi, w_lo = sb("w_out_hi", [P, KC, D], F32R), sb("w_out_lo", [P, KC, D], F32R)
        m_raw = [sb(f"m_raw{b}", [P, KC, OT]) for b in range(2)]
        m_hi = [sb(f"m_hi{b}", [P, KC, OT], F32R) for b in range(2)]
        m_lo = [sb(f"m_lo{b}", [P, KC, OT], F32R) for b in range(2)]
        x = [sb(f"x_res{b}", [P, D]) for b in range(2)]
        normed = [sb(f"o_normed{b}", [P, D]) for b in range(2)]
        result = [sb(f"o_result{b}", [P, D]) for b in range(2)]
        squares = sb("o_squares", [P, D])
        post_g = sb("post_g", [P, D])
        ssum = [sb(f"o_ssum{b}", [P, 1]) for b in range(2)]
        std = [sb(f"o_std{b}", [P, 1]) for b in range(2)]
        rinv = [sb(f"o_rinv{b}", [P, 1]) for b in range(2)]
        acc = [ctx.enter_context(nc.psum_tensor(f"oo{b}", [P, D], F32)) for b in range(2)]
        g_in, w_high, w_low = sem("o_g_in"), sem("o_w_high"), sem("o_w_low")
        w_in = sem("o_w_in")
        m_in = [sem(f"o_m_in{b}") for b in range(2)]
        x_in = [sem(f"o_x_in{b}") for b in range(2)]
        sent = [sem(f"o_sent{b}") for b in range(2)]
        m_high, m_low, product = sem("o_m_high"), sem("o_m_low"), sem("o_product")
        summed, rooted, inverted, scaled, added = sem("o_summed"), sem("o_rooted"), sem("o_inverted"), sem("o_scaled"), sem("o_added")
        block = ctx.enter_context(nc.Block())
        TILES = SEQ // P
        GROUPS_O = SEQ // OT

        def raw(k):
            return w_first[:, k, :] if k < KC // 2 else w_second[:, k - KC // 2, :]

        @block.sync
        def _(sp):
            def load(j, b):
                sp.dma_start(m_raw[b][:, :, :], scratch["mixed"][:, bass.ds(OT * j, OT)].rearrange(
                    "(k p) c -> p k c", p=P)).then_inc(m_in[b], 16)

            load(0, 0)
            sp.dma_start(w_second[:, :, :], io["w_out"][D // 2:, :].rearrange("(k p) c -> p k c", p=P)).then_inc(w_in, 16)
            sp.dma_start(x[0][:, :], io["x"][0:P, :]).then_inc(x_in[0], 16)
            sp.dma_start(post_g[:, :], io["post_norm_g"].broadcast_to([P, D])).then_inc(g_in, 16)
            load(1, 1)
            sp.dma_start(x[1][:, :], io["x"][P:2 * P, :]).then_inc(x_in[1], 16)
            with sp.Fori(0, GROUPS_O // 2 - 1) as i:
                for b in range(2):
                    for u in range(2):
                        sp.wait_ge(added, 4 * i + 2 * b + u + 1)
                        sp.dma_start(x[u][:, :], io["x"][bass.ds(P * (4 * i + 2 * b + u + 2), P), :]).then_inc(x_in[u], 16)
                    load(2 * i + b + 2, b)
            for u in range(2):
                sp.wait_ge(added, TILES - 4 + u + 1)
                sp.dma_start(x[u][:, :], io["x"][P * (TILES - 2 + u):P * (TILES - 1 + u), :]).then_inc(x_in[u], 16)

        @block.scalar
        def _(act):
            def split(j, b):
                act.wait_ge(m_in[b], 16 * ((j - b) // 2) + 16)
                act.copy(m_hi[b][:, :, :], m_raw[b][:, :, :]).then_inc(m_high, 1)

            def norm(n, u):
                act.wait_ge(product, n + 1)
                act.activation(squares[:, :], acc[u][:, :], ACT.Square, accum_out=ssum[u][:, :]).then_inc(summed, 1)
                act.wait_ge(summed, n + 1)
                act.activation(std[u][:, :], ssum[u][:, :], ACT.Sqrt, scale=1.0 / D, bias=t["eps"][:, 0:1]).then_inc(rooted, 1)

            def store(n, u):
                act.wait_ge(added, n + 1)
                act.dma_start(out[bass.ds(P * n, P), :], result[u][:, :]).then_inc(sent[u], 16)

            for u in range(2):
                act.sem_inc(sent[u], 16)
            split(0, 0)
            for k in range(KC):
                if k == KC // 2:
                    act.wait_ge(w_in, 16)
                act.copy(w_hi[:, k, :], raw(k)).then_inc(w_high, 1)
            norm(0, 0)
            split(1, 1)
            norm(1, 1)
            store(0, 0)
            with act.Fori(0, GROUPS_O // 2 - 1) as i:
                for b in range(2):
                    n = 4 * i + 2 * b + 2
                    norm(n, 0)
                    store(n - 1, 1)
                    split(2 * i + b + 2, b)
                    norm(n + 1, 1)
                    store(n, 0)
            n = TILES - 2
            norm(n, 0)
            store(n - 1, 1)
            norm(n + 1, 1)
            store(n, 0)
            store(n + 1, 1)
            for u in range(2):
                act.wait_ge(sent[u], 16 * (TILES // 2) + 16)

        @block.tensor
        def _(pe):
            pe.wait_ge(w_low, KC)
            with pe.Fori(0, GROUPS_O // 2) as i:
                for b in range(2):
                    pe.wait_ge(m_low, 2 * i + b + 1)
                    for u in range(2):
                        n = 4 * i + 2 * b + u
                        pe.wait_ge(scaled, n + 1)
                        tok = slice(P * u, P * u + P)
                        for half in range(2):
                            cols = slice(512 * half, 512 * half + 512)
                            for k in range(KC):
                                dst = acc[u][:, cols]
                                pe.matmul(dst, m_hi[b][:, k, tok], w_hi[:, k, cols], start=k == 0, stop=False)
                                pe.matmul(dst, m_hi[b][:, k, tok], w_lo[:, k, cols], start=False, stop=False)
                                mm = pe.matmul(dst, m_lo[b][:, k, tok], w_hi[:, k, cols], start=False, stop=k == KC - 1)
                        mm.then_inc(product, 1)

        @block.vector
        def _(dve):
            def split(j, b):
                dve.wait_ge(m_high, j + 1)
                dve.tensor_tensor(m_lo[b][:, :, :], m_raw[b][:, :, :], m_hi[b][:, :, :].bitcast(F32),
                                  ALU.subtract).then_inc(m_low, 1)

            def norm(n, u):
                dve.wait_ge(rooted, n + 1)
                dve.reciprocal(rinv[u][:, :], std[u][:, :]).then_inc(inverted, 1)
                dve.wait_ge(inverted, n + 1)
                if not isinstance(n, int) or n >= 2:
                    dve.wait_ge(added, n - 1)
                dve.scalar_tensor_tensor(normed[u][:, :], acc[u][:, :], rinv[u][:, 0:1], post_g[:, :], ALU.mult,
                                         ALU.mult).then_inc(scaled, 1)

            split(0, 0)
            for k in range(KC):
                dve.wait_ge(w_high, k + 1)
                dve.tensor_tensor(w_lo[:, k, :], raw(k), w_hi[:, k, :].bitcast(F32),
                                  ALU.subtract).then_inc(w_low, 1)
            dve.wait_ge(g_in, 16)
            dve.sem_inc(scaled, 2)
            norm(0, 0)
            split(1, 1)
            norm(1, 1)
            with dve.Fori(0, GROUPS_O // 2 - 1) as i:
                for b in range(2):
                    n = 4 * i + 2 * b + 2
                    norm(n, 0)
                    split(2 * i + b + 2, b)
                    norm(n + 1, 1)
            norm(TILES - 2, 0)
            norm(TILES - 1, 1)

        @block.gpsimd
        def _(pool):
            with pool.Fori(0, TILES // 2) as i:
                for u in range(2):
                    n = 2 * i + u
                    pool.wait_ge(scaled, n + 3)
                    pool.wait_ge(x_in[u], 16 * i + 16)
                    pool.wait_ge(sent[u], 16 * i + 16)
                    pool.tensor_tensor(result[u][:, :], normed[u][:, :], x[u][:, :], ALU.add).then_inc(added, 1)

def program(nc, io, out):
    with ExitStack() as ctx:
        taken = []

        def sem(name):
            taken.append(nc.alloc_semaphore(name))
            return taken[-1]

        dram = lambda name, shape: nc.dram_tensor("scr_" + name, shape, F32, kind="Internal").ap()
        scratch = {
            "u": dram("u", (3 * D + P, 1 + TOK)),
            "qk": dram("qk", (2 * D, TOK)),
            "v_sb": dram("v_sb", (TOK, D)),
            "gates": dram("gates", (2 * D, SEQ)),
            "merge": dram("merge", (2 * D, SEQ)),
            "y": dram("y", (2 * D, SEQ)),
            "mixed": dram("mixed", (D, SEQ)),
        }
        sb = lambda name, shape, dt=F32: ctx.enter_context(nc.sbuf_tensor(name, shape, dt))
        t = {"identity": sb("t_identity", [P, P]), "pre_g": sb("t_pre_g", [P, KC]), "eps": sb("t_eps", [P, 2])}
        with ExitStack() as held:
            for part in ("hn_hi", "hn_lo"):
                t[part] = held.enter_context(nc.sbuf_tensor(part, [P, KC, TOK], F32R))
            norm_phase(nc, sem, t, io)
            project_phase(nc, sem, t, io, scratch)
        attention_phase(nc, sem, t, io, scratch)
        rwkv_phase(nc, sem, t, io, scratch)
        nc.clear_and_free_semaphores(taken)
        nc.all_engine_barrier()
        w_out_first = sb("w_out_first", [P, KC // 2, D])
        branch_phase(nc, sem, t, io, scratch, w_out_first)
        output_phase(nc, sem, t, io, out, scratch, w_out_first)


def kernel(x, meta_tokens, pre_norm_g, post_norm_g, w_in, rwkv_mu, rwkv_w0, rwkv_w_up, rwkv_a0, rwkv_a_up,
           rwkv_k_k, rwkv_k_a, rwkv_r_k, rwkv_gn_g, rwkv_gn_b, w_proj_rwkv, w_proj_sb, w_out):
    import numpy as np
    import concourse.bacc as bacc
    from concourse.bass_utils import run_bass_kernel_spmd

    def channels(a):
        return a.reshape(-1, P).T

    shift, lora = 3 * D, P
    main = np.concatenate([w_in[0][:, :shift], w_in[0][:, shift + lora:]], axis=1)
    w_main = main.reshape(KC, P, -1, WB).transpose(2, 1, 0, 3).reshape(-1, P, KC * WB)
    w_lora = np.zeros((KC, P, WB), w_in.dtype)
    w_lora[:, :, :lora] = w_in[0][:, shift:shift + lora].reshape(KC, P, lora)
    params = np.concatenate([channels(rwkv_mu[0])] + [channels(a[0]) for a in (
        rwkv_w0, rwkv_a0, rwkv_k_k, rwkv_k_a, rwkv_r_k, rwkv_gn_g, rwkv_gn_b)], axis=1)

    j, i = np.arange(CHUNK)[:, None], np.arange(CHUNK)[None, :]
    joins = [((j // (2 * s) == i // (2 * s)) & (j // s < i // s)) for s in [1] + LEVELS]
    tri = np.concatenate([np.kron(np.eye(2), join) for join in joins], axis=1)
    before, upto = j < i, j <= i
    full = np.block([[before, upto], [np.zeros_like(before), upto]])
    restart = np.ones((P, PAIRS, CHUNK))
    restart[:, :, 0] = 0
    q, k = np.arange(P)[:, None], np.arange(P)[None, :]
    f32 = lambda a: np.ascontiguousarray(np.asarray(a, np.float32))
    given = {
        "x": x[0], "meta_tokens": meta_tokens, "pre_norm_g": channels(pre_norm_g[0]), "post_norm_g": post_norm_g,
        "w_main": w_main, "w_lora": w_lora.transpose(1, 0, 2).reshape(P, -1), "params": params,
        "up": np.concatenate([rwkv_w_up[0], rwkv_a_up[0]], axis=0),
        "w_proj": np.concatenate([w_proj_rwkv[0], w_proj_sb[0]], axis=0), "w_out": w_out[0],
    }
    constants = {
        "identity": f32(np.eye(P)), "hidden": f32(np.where(k >= q, HIDDEN, 0)), "last_row": f32(q != P - 1),
        "tri": f32(tri), "full": f32(full),
        "ones_sum": f32(np.kron(np.eye(2), np.ones((DH, DH)))), "restart": f32(restart.reshape(P, -1)),
    }
    nc = bacc.Bacc("TRN2", target_bir_lowering=False, num_devices=1)
    arrays, io = {}, {}
    for name, a in {**given, **constants}.items():
        arrays["in_" + name] = np.ascontiguousarray(a)
        io[name] = nc.dram_tensor("in_" + name, a.shape, mybir.dt.from_np(a.dtype), kind="ExternalInput").ap()
    out = nc.dram_tensor("out", (SEQ, D), F32, kind="ExternalOutput").ap()
    program(nc, io, out)
    result = run_bass_kernel_spmd(nc, [arrays], core_ids=[0])
    return result.results[0]["out"].reshape(1, SEQ, D)
```
